# Optimizing a Trainium2 kernel written in Bass

```python
import math
import jax, jax.numpy as jnp
from jax import lax
import numpy as np

D_MODEL = 2048
BATCH = 1
SEQ = 256
DEPTH = 2

HEAD_DIM = 128
H_FOX = 6
H_DSA = 6
H_MEM = 4
D_FOX = H_FOX * HEAD_DIM
D_DSA = H_DSA * HEAD_DIM
D_MEMG = H_MEM * HEAD_DIM
D_MIX = D_FOX + D_DSA + D_MEMG
IDX_HEADS = 16
IDX_DIM = 64
INDEX_TOPK = 256
N_MEM = 256
Q_BLOCK = 128
ROPE_THETA = 10000.0
LN_EPS = 1e-5
ALPHA = (2 * DEPTH) ** 0.25
BETA = (8 * DEPTH) ** -0.25
NEG = -1e30

SPLITS = (
    D_FOX, D_FOX, D_FOX, D_FOX, H_FOX,
    D_DSA, D_DSA, D_DSA, D_DSA,
    IDX_HEADS * IDX_DIM, IDX_DIM, IDX_HEADS,
    D_MEMG, D_MEMG,
)
N_IN = sum(SPLITS)


def rope(x, pos):
    d = x.shape[-1]
    half = d // 2
    inv_freq = ROPE_THETA ** (-jnp.arange(half, dtype=jnp.float32) / half)
    ang = pos.astype(jnp.float32)[:, None] * inv_freq[None, :]
    cos = jnp.cos(ang)[None, :, None, :].astype(x.dtype)
    sin = jnp.sin(ang)[None, :, None, :].astype(x.dtype)
    x1, x2 = x[..., :half], x[..., half:]
    return jnp.concatenate([x1 * cos - x2 * sin, x2 * cos + x1 * sin], axis=-1)

def to_blocks(a):
    b, s = a.shape[0], a.shape[1]
    return jnp.moveaxis(a.reshape(b, s // Q_BLOCK, Q_BLOCK, *a.shape[2:]), 1, 0)

def from_blocks(a):
    a = jnp.moveaxis(a, 0, 1)
    return a.reshape(a.shape[0], a.shape[1] * a.shape[2], *a.shape[3:])

def fox_attention(q, k, v, cum_logf):
    b, s, h, d = q.shape
    scale = d ** -0.5
    key_pos = jnp.arange(s)
    c_keys = jnp.transpose(cum_logf, (0, 2, 1))
    q_pos = key_pos.reshape(s // Q_BLOCK, Q_BLOCK)

    def one_block(args):
        qb, cb, tb = args
        sc = jnp.einsum('bqhd,bkhd->bhqk', qb, k).astype(jnp.float32) * scale
        sc = sc + (jnp.transpose(cb, (0, 2, 1))[:, :, :, None] - c_keys[:, :, None, :])
        causal = tb[:, None] >= key_pos[None, :]
        sc = jnp.where(causal[None, None], sc, NEG)
        p = jax.nn.softmax(sc, axis=-1).astype(v.dtype)
        return jnp.einsum('bhqk,bkhd->bqhd', p, v)

    out = lax.map(one_block, (to_blocks(q), to_blocks(cum_logf), q_pos))
    return from_blocks(out)

def dsa_attention(q, k, v, q_idx, k_idx, w_idx):
    b, s, h, d = q.shape
    topk = min(INDEX_TOPK, s // 4)
    scale = d ** -0.5
    idx_scale = IDX_DIM ** -0.5
    key_pos = jnp.arange(s)
    q_pos = key_pos.reshape(s // Q_BLOCK, Q_BLOCK)

    def one_block(args):
        qb, qib, wb, tb = args
        rel = jax.nn.relu(jnp.einsum('bqhi,bki->bqhk', qib, k_idx).astype(jnp.float32) * idx_scale)
        score = jnp.einsum('bqhk,bqh->bqk', rel, wb.astype(jnp.float32))
        causal = tb[:, None] >= key_pos[None, :]
        score = jnp.where(causal[None], score, NEG)
        _, sel = lax.top_k(score, topk)
        valid = sel <= tb[None, :, None]
        kg = jax.vmap(lambda kk, ii: kk[ii])(k, sel)
        vg = jax.vmap(lambda vv, ii: vv[ii])(v, sel)
        sc = jnp.einsum('bqhd,bqkhd->bhqk', qb, kg).astype(jnp.float32) * scale
        sc = jnp.where(jnp.transpose(valid, (0, 1, 2))[:, None], sc, NEG)
        p = jax.nn.softmax(sc, axis=-1).astype(vg.dtype)
        return jnp.einsum('bhqk,bqkhd->bqhd', p, vg)

    out = lax.map(one_block, (to_blocks(q), to_blocks(q_idx), to_blocks(w_idx), q_pos))
    return from_blocks(out)

def memory_attention(q, k_mem, v_mem):
    scale = q.shape[-1] ** -0.5
    sc = jnp.einsum('bshd,bmhd->bhsm', q, k_mem).astype(jnp.float32) * scale
    p = jax.nn.softmax(sc, axis=-1).astype(v_mem.dtype)
    return jnp.einsum('bhsm,bmhd->bshd', p, v_mem)

def layer_norm(z, g, b):
    zf = z.astype(jnp.float32)
    mu = jnp.mean(zf, axis=-1, keepdims=True)
    var = jnp.mean(jnp.square(zf - mu), axis=-1, keepdims=True)
    out = (zf - mu) * lax.rsqrt(var + LN_EPS) * g.astype(jnp.float32) + b.astype(jnp.float32)
    return out.astype(z.dtype)

def hybrid_layer(x, mem, w_in, b_forget, w_mem_kv, w_out, ln_gain, ln_bias):
    b, s, _ = x.shape
    pos = jnp.arange(s)
    h = jnp.einsum('bsd,dn->bsn', x, w_in)
    offsets = np.cumsum(SPLITS)[:-1].tolist()
    (fq, fk, fv, fg, f_logit,
     dq, dk, dv, dg,
     iq, ik, iw,
     mq, mg) = jnp.split(h, offsets, axis=-1)

    heads = lambda t, nh: t.reshape(b, s, nh, HEAD_DIM)

    log_f = jax.nn.log_sigmoid(f_logit.astype(jnp.float32) + b_forget.astype(jnp.float32))
    cum_logf = jnp.cumsum(log_f, axis=1)
    y_fox = fox_attention(heads(fq, H_FOX), heads(fk, H_FOX), heads(fv, H_FOX), cum_logf)
    y_fox = y_fox.reshape(b, s, D_FOX) * jax.nn.silu(fg)

    q_idx = rope(iq.reshape(b, s, IDX_HEADS, IDX_DIM), pos)
    k_idx = rope(ik.reshape(b, s, 1, IDX_DIM), pos)[:, :, 0, :]
    w_idx = iw * (IDX_HEADS ** -0.5)
    y_dsa = dsa_attention(rope(heads(dq, H_DSA), pos), rope(heads(dk, H_DSA), pos), heads(dv, H_DSA),
                          q_idx, k_idx, w_idx)
    y_dsa = y_dsa.reshape(b, s, D_DSA) * jax.nn.silu(dg)

    kv = jnp.einsum('bmd,dn->bmn', mem, w_mem_kv)
    k_mem, v_mem = jnp.split(kv, 2, axis=-1)
    m = mem.shape[1]
    y_mem = memory_attention(heads(mq, H_MEM), k_mem.reshape(b, m, H_MEM, HEAD_DIM),
                             v_mem.reshape(b, m, H_MEM, HEAD_DIM))
    y_mem = y_mem.reshape(b, s, D_MEMG) * jax.nn.silu(mg)

    y = jnp.concatenate([y_fox, y_dsa, y_mem], axis=-1)
    y = jnp.einsum('bsn,nd->bsd', y, w_out)
    return layer_norm(ALPHA * x + y, ln_gain, ln_bias)

def first_inputs(seed: int = 0) -> dict:
    key = jax.random.key(seed)
    ks = jax.random.split(key, 8)
    x = jax.random.normal(ks[0], (BATCH, SEQ, D_MODEL), jnp.float32)
    mem = jax.random.normal(ks[1], (BATCH, N_MEM, D_MODEL), jnp.float32)
    w_in = jax.random.normal(ks[2], (DEPTH, D_MODEL, N_IN), jnp.float32) * D_MODEL ** -0.5
    b_forget = 3.0 + 0.5 * jax.random.normal(ks[3], (DEPTH, H_FOX), jnp.float32)
    w_mem_kv = jax.random.normal(ks[4], (DEPTH, D_MODEL, 2 * D_MEMG), jnp.float32) * D_MODEL ** -0.5
    w_out = jax.random.normal(ks[5], (DEPTH, D_MIX, D_MODEL), jnp.float32) * (D_MIX ** -0.5) * BETA
    ln_gain = 1.0 + 0.05 * jax.random.normal(ks[6], (DEPTH, D_MODEL), jnp.float32)
    ln_bias = 0.02 * jax.random.normal(ks[7], (DEPTH, D_MODEL), jnp.float32)
    return {"x": x, "mem": mem, "w_in": w_in, "b_forget": b_forget, "w_mem_kv": w_mem_kv,
            "w_out": w_out, "ln_gain": ln_gain, "ln_bias": ln_bias}

def first_block(x, mem, w_in, b_forget, w_mem_kv, w_out, ln_gain, ln_bias):
    h = x
    for l in range(DEPTH):
        h = hybrid_layer(h, mem, w_in[l], b_forget[l], w_mem_kv[l], w_out[l], ln_gain[l], ln_bias[l])
    return h


DEPTH_2 = 1

N_ATTN_HEADS = 8
ATTN_WIDTH = N_ATTN_HEADS * HEAD_DIM
CONV_CHANNELS = D_MODEL - ATTN_WIDTH
CONV_GROUPS = 8
MIX_WIDTH = ATTN_WIDTH + CONV_CHANNELS
IN_COLS = 3 * ATTN_WIDTH + 2 * CONV_CHANNELS
MOBA_BLOCK = 256
MOBA_TOPK = 3
Q_CHUNK = 64
CONV_WIDTH = 31
D_FF = 4 * D_MODEL
RMS_EPS = 1e-6


def rms_norm(x, g):
    xf = x.astype(jnp.float32)
    y = xf * lax.rsqrt(jnp.mean(xf * xf, axis=-1, keepdims=True) + RMS_EPS)
    return (y * g.astype(jnp.float32)).astype(x.dtype)

def layer_norm_2(x, g, b):
    xf = x.astype(jnp.float32)
    mu = jnp.mean(xf, axis=-1, keepdims=True)
    var = jnp.mean(jnp.square(xf - mu), axis=-1, keepdims=True)
    y = (xf - mu) * lax.rsqrt(var + LN_EPS)
    return (y * g.astype(jnp.float32) + b.astype(jnp.float32)).astype(x.dtype)

def alibi_slopes(n_heads):
    return jnp.asarray(2.0 ** (-8.0 * np.arange(1, n_heads + 1) / n_heads), dtype=jnp.float32)

def moba_attention(q, k, v):
    B, H, S, Dh = q.shape
    L = MOBA_BLOCK
    n_blocks = -(-S // L)
    pad = n_blocks * L - S
    kp = jnp.pad(k, ((0, 0), (0, 0), (0, pad), (0, 0)))
    vp = jnp.pad(v, ((0, 0), (0, 0), (0, pad), (0, 0)))
    k_blk = kp.reshape(B, H, n_blocks, L, Dh)
    v_blk = vp.reshape(B, H, n_blocks, L, Dh)
    k_mean = jnp.mean(k_blk.astype(jnp.float32), axis=3)
    topk = min(MOBA_TOPK, n_blocks)
    scale = Dh ** -0.5
    slopes = alibi_slopes(H)
    n_chunks = S // Q_CHUNK
    q_chunks = q.reshape(B, H, n_chunks, Q_CHUNK, Dh).transpose(2, 0, 1, 3, 4)
    gather = jax.vmap(jax.vmap(lambda blocks, idx: blocks[idx]))
    neg_inf = -jnp.inf

    def chunk_fn(args):
        c, qc = args
        q0 = c * Q_CHUNK
        blk = q0 // L
        q_pos = q0 + jnp.arange(Q_CHUNK)
        gate = jnp.einsum('bhqd,bhnd->bhqn', qc.astype(jnp.float32), k_mean)
        gate = jnp.where(jnp.arange(n_blocks) < blk, gate, neg_inf)
        _, sel = lax.top_k(gate, topk)
        sel_valid = jnp.arange(topk) < blk
        k_sel = gather(k_blk, sel)
        v_sel = gather(v_blk, sel)
        s_sel = jnp.einsum('bhqd,bhqrld->bhqrl', qc, k_sel,
                           preferred_element_type=jnp.float32) * scale
        k_pos_sel = sel[..., None] * L + jnp.arange(L)
        dist_sel = jnp.abs(q_pos[None, None, :, None, None] - k_pos_sel).astype(jnp.float32)
        s_sel = jnp.where(sel_valid[:, None],
                          s_sel - slopes[None, :, None, None, None] * dist_sel, neg_inf)
        k_own = lax.dynamic_slice_in_dim(kp, blk * L, L, axis=2)
        v_own = lax.dynamic_slice_in_dim(vp, blk * L, L, axis=2)
        s_own = jnp.einsum('bhqd,bhld->bhql', qc, k_own,
                           preferred_element_type=jnp.float32) * scale
        k_pos_own = blk * L + jnp.arange(L)
        dist_own = jnp.abs(q_pos[:, None] - k_pos_own[None, :]).astype(jnp.float32)
        causal = k_pos_own[None, :] <= q_pos[:, None]
        s_own = jnp.where(causal, s_own - slopes[:, None, None] * dist_own, neg_inf)
        s = jnp.concatenate([s_sel.reshape(B, H, Q_CHUNK, topk * L), s_own], axis=-1)
        p = jax.nn.softmax(s, axis=-1)
        p_sel = p[..., :topk * L].reshape(B, H, Q_CHUNK, topk, L).astype(v.dtype)
        p_own = p[..., topk * L:].astype(v.dtype)
        out = (jnp.einsum('bhqrl,bhqrld->bhqd', p_sel, v_sel, preferred_element_type=jnp.float32)
               + jnp.einsum('bhql,bhld->bhqd', p_own, v_own, preferred_element_type=jnp.float32))
        return out.astype(qc.dtype)

    out = lax.map(chunk_fn, (jnp.arange(n_chunks), q_chunks))
    return out.transpose(1, 0, 3, 2, 4).reshape(B, S, H * Dh)

def conformer_conv(u, b_glu, w_dw, b_dw, ln_g, ln_b):
    u = u + b_glu
    val, gt = jnp.split(u, 2, axis=-1)
    h = val * jax.nn.sigmoid(gt)
    C = h.shape[-1]
    rhs = w_dw.reshape(CONV_WIDTH, 1, C)
    y = lax.conv_general_dilated(h, rhs, window_strides=(1,),
                                 padding=[(CONV_WIDTH - 1, 0)],
                                 dimension_numbers=('NWC', 'WIO', 'NWC'),
                                 feature_group_count=C)
    y = layer_norm_2(y + b_dw, ln_g, ln_b)
    return jax.nn.silu(y)

def second_inputs(seed: int = 0) -> dict:
    key = jax.random.key(seed)
    ks = jax.random.split(key, 14)
    f32 = jnp.float32

    def nrm(k, shape, scale):
        return jax.random.normal(k, shape, f32) * scale

    def gain(k, shape):
        return 1.0 + 0.02 * jax.random.normal(k, shape, f32)

    return {
        'x': nrm(ks[0], (BATCH, SEQ, D_MODEL), 1.0),
        'g_mix_pre': gain(ks[1], (DEPTH_2, D_MODEL)),
        'w_in': nrm(ks[2], (DEPTH_2, D_MODEL, IN_COLS), D_MODEL ** -0.5),
        'b_glu': nrm(ks[3], (DEPTH_2, 2 * CONV_CHANNELS), 0.02),
        'w_dw': nrm(ks[4], (DEPTH_2, CONV_WIDTH, CONV_CHANNELS), CONV_WIDTH ** -0.5),
        'b_dw': nrm(ks[5], (DEPTH_2, CONV_CHANNELS), 0.02),
        'ln_conv_g': gain(ks[6], (DEPTH_2, CONV_CHANNELS)),
        'ln_conv_b': nrm(ks[7], (DEPTH_2, CONV_CHANNELS), 0.02),
        'w_out': nrm(ks[8], (DEPTH_2, MIX_WIDTH, D_MODEL), MIX_WIDTH ** -0.5),
        'g_mix_post': gain(ks[9], (DEPTH_2, D_MODEL)),
        'g_ffn_pre': gain(ks[10], (DEPTH_2, D_MODEL)),
        'w_ff1': nrm(ks[11], (DEPTH_2, D_MODEL, D_FF), D_MODEL ** -0.5),
        'w_ff2': nrm(ks[12], (DEPTH_2, D_FF, D_MODEL), D_FF ** -0.5),
        'g_ffn_post': gain(ks[13], (DEPTH_2, D_MODEL)),
    }

def second_block(x, g_mix_pre, w_in, b_glu, w_dw, b_dw, ln_conv_g, ln_conv_b, w_out,
              g_mix_post, g_ffn_pre, w_ff1, w_ff2, g_ffn_post):
    B, S, _ = x.shape
    h = x
    for l in range(DEPTH_2):
        a = rms_norm(h, g_mix_pre[l])
        proj = a @ w_in[l]
        q = proj[..., :ATTN_WIDTH]
        k = proj[..., ATTN_WIDTH:2 * ATTN_WIDTH]
        v = proj[..., 2 * ATTN_WIDTH:3 * ATTN_WIDTH]
        u = proj[..., 3 * ATTN_WIDTH:]
        to_heads = lambda t: t.reshape(B, S, N_ATTN_HEADS, HEAD_DIM).transpose(0, 2, 1, 3)
        attn = moba_attention(to_heads(q), to_heads(k), to_heads(v))
        conv = conformer_conv(u, b_glu[l], w_dw[l], b_dw[l], ln_conv_g[l], ln_conv_b[l])
        mixed = jnp.concatenate([attn, conv], axis=-1) @ w_out[l]
        h = h + rms_norm(mixed, g_mix_post[l])
        f = rms_norm(h, g_ffn_pre[l])
        f = jnp.square(jax.nn.relu(f @ w_ff1[l])) @ w_ff2[l]
        h = h + rms_norm(f, g_ffn_post[l])
    return h


def setup_inputs(seed=0):
    out = dict(first_inputs(seed))
    for name, value in second_inputs(seed + 1).items():
        if name != "x":
            out[name + "_2"] = value
    return out


def reference(
    x, mem, w_in, b_forget, w_mem_kv, w_out, ln_gain, ln_bias, g_mix_pre_2, w_in_2, b_glu_2,
    w_dw_2, b_dw_2, ln_conv_g_2, ln_conv_b_2, w_out_2, g_mix_post_2, g_ffn_pre_2, w_ff1_2,
    w_ff2_2, g_ffn_post_2,
):
    x = first_block(
        x, mem, w_in, b_forget, w_mem_kv, w_out, ln_gain, ln_bias,
    )
    return second_block(
        x, g_mix_pre_2, w_in_2, b_glu_2, w_dw_2, b_dw_2, ln_conv_g_2, ln_conv_b_2, w_out_2,
        g_mix_post_2, g_ffn_pre_2, w_ff1_2, w_ff2_2, g_ffn_post_2,
    )


_drawn_inputs = setup_inputs


def setup_inputs(seed=0):
    import zlib

    import numpy as np

    out = dict(_drawn_inputs(seed))
    spreads = {}
    factors = {'mem': 3.115,
     'w_mem_kv': 3.066,
     'g_mix_pre_2': 3.09,
     'b_glu_2': 3.892,
     'ln_conv_g_2': 40.175,
     'ln_conv_b_2': 37.521,
     'g_mix_post_2': 10.23,
     'g_ffn_pre_2': 35.426,
     'g_ffn_post_2': 56.217,
     'b_dw_2': 6.479}
    for name, (base, spread) in spreads.items():
        noise = np.random.default_rng([zlib.crc32(name.encode()), seed]).standard_normal(out[name].shape)
        drawn = base * np.exp(spread * noise) if base else spread * noise
        out[name] = __import__('jax').numpy.asarray(drawn.astype(out[name].dtype))
    for name, factor in factors.items():
        out[name] = (out[name] * factor).astype(out[name].dtype)
    return out
```

```python
from contextlib import ExitStack

import numpy as np

import concourse.bass as bass
from concourse import mybir

F32 = mybir.dt.float32
F32R = mybir.dt.float32r
ACT = mybir.ActivationFunctionType
ALU = mybir.AluOpType
AXX = mybir.AxisListType.X

P = 128
S = 256
ST = S // P
D = 2048
KT = D // P
DEPTH = 2
HD = 128
HF, HS, HM = 6, 6, 4
NJOB = HF + HS + HM
IH, IDIM = 16, 64
TOPK = min(256, S // 4)
H2 = 8
CONV = 1024
TAPS = 31
PAD = TAPS - 1
DFF = 8192
NQ = 4
ALPHA = (2 * DEPTH) ** 0.25
SCALE = HD ** -0.5
LN_EPS, RMS_EPS = 1e-5, 1e-6
BIG = 1e30
TAKEN = -3e38
RING = 4
LEAD = 2
CW = 512
KB = D // 256

C_FQ, C_FV, C_FL = 0, 1536, 3072
C_DQ, C_DV, C_IQ, C_IK = 3078, 4614, 6150, 7174
C_MQ, C_MG = 7254, 7766
NAR = IDIM + IH + HF


class Chunk:

    def __init__(self, name, w, rows, col, width, seg=None, acc=None, kts=None):
        self.name, self.w, self.rows, self.col, self.width, self.seg = name, w, rows, col, width, seg
        self.acc = acc
        self.kts = kts if kts is not None else [2 * i for i in range(len(rows))]
        self.g0 = None


def plan(a):
    order, by = [], {}
    state = {"g": 0, "acc": 0}

    def add(key, w, col, rows=None, width=CW, seg=None, narrow=False, kts=None):
        c = Chunk(key, w, rows or [256 * i for i in range(KB)], col, width, seg, kts=kts)
        c.g0 = state["g"]
        state["g"] += len(c.rows)
        c.end = state["g"]
        if not narrow:
            c.acc = state["acc"]
            state["acc"] += 1
        order.append(c)
        by[key] = c

    for l in range(DEPTH):
        for i in range(2):
            add(("mem", l, i), a["w_mem_kv"][l], 512 * i)
    for l in range(DEPTH):
        w = a["w_in"][l]
        add(("nar", l), w, C_IK, width=NAR, narrow=True)
        for m in range(3):
            add(("qk", l, m), w, C_FQ + 256 * m, seg=768)
        for m in range(3):
            add(("vg", l, m), w, C_FV + 512 * m)
        for m in range(2):
            add(("iq", l, m), w, C_IQ + 512 * m)
        for m in range(3):
            add(("dvg", l, m), w, C_DV + 512 * m)
        add(("mq", l), w, C_MQ)
        for m in range(3):
            add(("dqk", l, m), w, C_DQ + 256 * m, seg=768)
        add(("mg", l), w, C_MG)
        for n in range(4):
            add(("o", l, n), a["w_out"][l], 512 * n)
    w = a["w_in_2"][0]
    for m in range(2):
        add(("val", m), w, 3072 + 512 * m)
        add(("gt", m), w, 4096 + 512 * m)
    for m in range(2):
        add(("v2", m), w, 2048 + 512 * m)
    for m in range(4):
        add(("qk2", m), w, 256 * m, seg=1024)
    w = a["w_out_2"][0]
    for n in range(4):
        add(("oa", n), w, 512 * n, rows=[0, 256, 512], kts=[0, 2, 4])
    for n in range(4):
        add(("ob", n), w, 512 * n, rows=[768 + 256 * i for i in range(5)], kts=[6 + 2 * i for i in range(5)])
    for q in range(NQ):
        for i in range(4):
            add(("f1", q, i), a["w_ff1_2"][0], D * q + 512 * i)
        for n in range(4):
            add(("f2", q, n), a["w_ff2_2"][0], 512 * n, rows=[D * q + 256 * i for i in range(KB)])
    return order, by


SCORES = {58 + h: ("fox", h) for h in range(HF)}
SCORES |= {108 + h: ("mem", h) for h in range(HM)}
SCORES |= {117 + 8 * (h // 2) + h % 2: ("dsa", h) for h in range(HS)}
SCORES2 = {60 + 8 * (h // 2) + h % 2: ("ali", h) for h in range(H2)}
LAYER_SLOTS, LAYER0 = 168, 32
BLOCK2, BLOCK2_SLOTS = LAYER0 + DEPTH * 168, 112
FF0, FF_SLOTS = BLOCK2 + 112, 64
IDX_AT, TOPK_AT, CONV_AT = 77, 83, 20
CONV_PER_SLOT = 4
CONV_OPS = 8 * TAPS
MEAN_AT, VAR_AT = 86, 88


def job_no(l, kind, h):
    return {"fox": 16 * l + h, "mem": 16 * l + HF + h, "dsa": 16 * l + HF + HM + h, "ali": 32 + h}[kind]


def tile_no(l, kind, h):
    return {"fox": 16 * l + h, "dsa": 16 * l + HF + h, "mem": 16 * l + HF + HS + h, "ali": 32 + h}[kind]


def offsets(sizes):
    at, out = 0, {}
    for name, n in sizes:
        out[name] = (at, at + n)
        at += n
    return out, at


CONST, N_CONST = offsets([("ident", P), ("mask", 3 * P), ("upto", S), ("cos", 2 * HD), ("sin", 2 * HD),
                          ("icos", 2 * IDIM), ("isin", 2 * IDIM), ("dist", 3 * P)])
PARAM, N_PARAM = offsets([("gain", DEPTH * KT), ("bias", DEPTH * KT), ("gpre", KT), ("gffn", KT),
                          ("bf", DEPTH * HF), ("bglu", KT), ("bdw", 8), ("cg", 8), ("cb", 8), ("wdw", 8 * TAPS)])


def build(nc, a, out):
    order, by = plan(a)
    with ExitStack() as ctx:
        def sb(name, shape, dt=F32):
            return ctx.enter_context(nc.sbuf_tensor(name, shape, dt))

        def sem(name):
            return ctx.enter_context(nc.semaphore(name))

        raw = sb("raw", [P, RING, 2, CW])
        high = sb("high", [P, RING, 2, CW], F32R)
        low = sb("low", [P, RING, 2, CW], F32R)
        xh = sb("xh", [P, KT, S], F32R)
        xl = sb("xl", [P, KT, S], F32R)
        with nc.sbuf_tensor("yhf", [P, KT, S], F32) as yhf:
            pass
        yh = sb("yh", [P, KT, S], F32R)
        with nc.sbuf_tensor("ylf", [P, KT, S], F32) as ylf:
            pass
        yl = sb("yl", [P, KT, S], F32R)
        x = sb("x_nat", [P, ST, D])
        work = sb("work", [P, 12528])
        cb = sb("cb", [P, 4, CW])
        sc = sb("sc", [P, 2, ST, S])
        pt = sb("pt", [P, 2, CW])
        y = sb("y", [P, 2, ST, HD])
        consts = sb("consts", [P, N_CONST])
        params = sb("params", [P, N_PARAM])
        nar = sb("nar", [P, ST, NAR])
        small = sb("small", [P, 384])

        acc = ctx.enter_context(nc.psum_tensor("acc", [P, 4, 512], F32))
        tb = ctx.enter_context(nc.psum_tensor("tb", [P, 2, 512], F32))
        sbank = ctx.enter_context(nc.psum_tensor("sbank", [P, 512], F32))
        obank = ctx.enter_context(nc.psum_tensor("obank", [P, 512], F32))

        def cut(t, at, *dims):
            n = int(np.prod(dims))
            v = t[:, at:at + n]
            if len(dims) == 2:
                v = v.rearrange("p (a b) -> p a b", a=dims[0])
            if len(dims) == 3:
                v = v.rearrange("p (a b c) -> p a b c", a=dims[0], b=dims[1])
            return v

        def flat(v):
            return v.rearrange("p a b -> p (a b)")

        def const(name, *dims):
            return cut(consts, CONST[name][0], *(dims or (CONST[name][1] - CONST[name][0],)))

        def param(name, i, n=1):
            at = PARAM[name][0] + i
            return params[:, at:at + n]

        ident, mask, upto = const("ident"), const("mask"), const("upto")
        tri = upto[:, 0:P]
        ones = upto[:, P:S]
        cos, sin = const("cos", ST, HD), const("sin", ST, HD)
        icos, isin = const("icos", ST, IDIM), const("isin", ST, IDIM)
        dist = const("dist")

        qT, kT = cut(work, 0, HF, S), cut(work, 1536, HF, S)
        vN, gN = cut(work, 3072, ST, 768), cut(work, 4608, ST, 768)
        mqT = cut(work, 6144, HM, S)
        kmT = [cut(work, 7168 + 1024 * l, HM, S) for l in range(DEPTH)]
        vm = [cut(work, 9216 + 1024 * l, ST, 512) for l in range(DEPTH)]
        ikT = cut(work, 11264, S)
        ndsa = cut(work, 11520, 512)
        q2T, k2T, v2 = cut(work, 0, H2, S), cut(work, 2048, H2, S), cut(work, 4096, ST, 1024)
        hT = cut(work, 8192, 8, PAD + S)
        hsq = cut(work, 8192, 8, S)
        cv = cut(work, 10480, 8, S)
        mixed = [cut(work, 6144, ST, CW), cut(work, 7168, ST, CW), cut(work, 0, ST, CW), cut(work, 2048, ST, CW)]
        rowp, rowf = cut(work, 4096, D), cut(work, 10480, D)
        yhw, ylw = yhf[:].rearrange("p a b -> p (a b)"), ylf[:].rearrange("p a b -> p (a b)")
        row_g, row_b = cut(yhw, 0, D), cut(yhw, D, D)
        iscore, itaken = cut(yhw, 6 * S, ST, S), cut(ylw, 6 * S, ST, S)
        iqT = cut(yhw, 8 * S, 8, S)
        nfox = cut(ylw, 8 * S, 3 * P)
        rot_b = cut(ylw, 10 * S, CW)
        ymem = cut(ylw, 12 * S, HM, ST, HD)
        chunkbuf = [cb[:, 2 * i:2 * i + 2, :] for i in range(2)]
        rel = [[cb[:, 2 * f + e, :] for e in range(2)] for f in range(2)]
        junk = pt[:, 0, :]
        cvar_b, cstd_b, crs_b, cnt_b = sc[:, 0, 0, :], sc[:, 0, 1, :], sc[:, 1, 0, :], sc[:, 1, 1, :]
        stage = [cb[:, i, :].rearrange("p (s c) -> p s c", s=ST) for i in range(2)]
        rot = [cb[:, 2 + i, :].rearrange("p (s c) -> p s c", s=ST) for i in range(2)]

        sm = {}
        sm_at = [0]

        def vec(name, n):
            sm[name] = small[:, sm_at[0]:sm_at[0] + n]
            sm_at[0] += n
            assert sm_at[0] <= 384
            return sm[name]

        mx, nmx, rs, rinv = (vec(k, 8) for k in ("mx", "nmx", "rs", "rinv"))
        stats = vec("stats", 48).rearrange("p (s c k) -> p s c k", s=ST, c=4)
        mv = vec("mv", 4).rearrange("p (s k) -> p s k", s=ST)
        var, std, rstd, nt = (vec(k, 2) for k in ("var", "std", "rstd", "nt"))
        rstd2, rstdm, rstd3, rstd4 = (vec(k, 2) for k in ("rstd2", "rstdm", "rstd3", "rstd4"))
        ssq = vec("ssq", 8).rearrange("p (s c) -> p s c", s=ST)
        fz, fe, fl, logf, cum = (vec(k, 12).rearrange("p (s h) -> p s h", s=ST) for k in ("fz", "fe", "fl", "logf", "cum"))
        wi = vec("wi", 32).rearrange("p (s h) -> p s h", s=ST)
        top8 = vec("top8", 16).rearrange("p (s k) -> p s k", s=ST)
        gb, bb = vec("gb", KT), vec("bb", KT)

        names = """s_in mem_landed x_landed rows_landed rowf_landed high_ready low_ready block_used s_full o_full
            m_ready p_ready pt_ready y_ready ym_ready yhi_ready yt_ready v_ready g_ready stage_ready rot_ready
            unit_ready nar_ready flog_in flog_e flog_ln logf_ready ikr_ready ikt_ready cum_ready decay_ready
            rel_ready rel_used hi_ready xt_ready var_ready std_ready norm_ready aff_ready sum_ready sq_ready
            xres_ready rs_ready cbuf_ready fsq_ready valT_ready sig_ready hT_ready conv_step yc_ready csq_ready
            cn_ready silu_ready ch_ready ct_ready fin_ready out_done dve_done""".split()
        sems = {n: sem(n) for n in names}
        (s_in, mem_landed, x_landed, rows_landed, rowf_landed, high_ready, low_ready, block_used, s_full, o_full,
         m_ready, p_ready, pt_ready, y_ready, ym_ready, yhi_ready, yt_ready, v_ready, g_ready, stage_ready, rot_ready,
         unit_ready, nar_ready, flog_in, flog_e, flog_ln, logf_ready, ikr_ready, ikt_ready, cum_ready, decay_ready,
         rel_ready, rel_used, hi_ready, xt_ready, var_ready, std_ready, norm_ready, aff_ready, sum_ready, sq_ready,
         xres_ready, rs_ready, cbuf_ready, fsq_ready, valT_ready, sig_ready, hT_ready, conv_step, yc_ready, csq_ready,
         cn_ready, silu_ready, ch_ready, ct_ready, fin_ready, out_done, dve_done) = (sems[n] for n in names)
        raw_landed = [sem(f"raw_landed{i}") for i in range(RING)]
        t_full = [sem(f"t_full{i}") for i in range(2)]

        t_no, s_no, o_no = {}, {}, {}

        def t_wait(eng, key):
            n = t_no[key]
            eng.wait_ge(t_full[n % 2], n // 2 + 1)
            return tb[:, n % 2, :]

        def accs(c):
            b = 2 * (c.acc % 2)
            return acc[:, b:b + 2, :]

        def slots(block, side, tail, g0, n):
            for b in range(n):
                block(g0 + b)
                if b >= LEAD:
                    side(b - LEAD)
            for b in range(n - LEAD, n):
                side(b)
            tail()

        chunk_at = {c.g0 + i: (c, i) for c in order for i in range(len(c.rows))}
        landed = {}
        for g in range(FF0 + NQ * FF_SLOTS):
            c = chunk_at[g][0]
            landed[g] = landed.get(g - RING, 0) + (32 if c.seg or c.name[0] == "nar" else 16)
        N_MEM_CHUNKS, LAYER_CHUNKS = 4, 21
        B2 = N_MEM_CHUNKS + DEPTH * LAYER_CHUNKS

        def pieces(l):
            return ([("qk", l, m, p) for m in range(3) for p in range(2)]
                    + [("iq", l, m, p) for m in range(2) for p in range(2)]
                    + [("mq", l, 0, p) for p in range(2)]
                    + [("dqk", l, m, p) for m in range(3) for p in range(2)])

        staged = [("mem", l, 0, p) for l in range(DEPTH) for p in range(2)]
        for l in range(DEPTH):
            staged += pieces(l) + [("mg", l, 0, p) for p in range(2)]
        stage_no = {k: n for n, k in enumerate(staged)}
        rot_no = {k: n for n, k in enumerate(k for k in staged if k[0] in ("iq", "dqk"))}
        units = [k for k in staged if k[0] != "mg"] + [("qk2", m, p) for m in range(4) for p in range(2)]
        unit_no = {k: n for n, k in enumerate(units)}

        def prev_chunk(l, b):
            i, kb = divmod(b, 8)
            return i, kb, order[N_MEM_CHUNKS + LAYER_CHUNKS * l + i - 1].name if i >= 1 else None

        def index_shape(f):
            return (0, P, range(8 * f, 8 * f + 8)) if f < 2 else (1, S, range(4 * (f - 2), 4 * (f - 2) + 4))

        block = ctx.enter_context(nc.Block())

        @block.tensor
        def _(pe):
            t_keys, s_keys, o_keys = [], [], []

            def t_released(key):
                k = key[0]
                if k in ("memT", "xT"):
                    pe.wait_ge(xt_ready, (8 if k == "xT" else 0) + key[1] + 1)
                elif k == "nT":
                    pe.wait_ge(aff_ready, 8 * key[1] + key[2] + 1)
                elif k == "h2T":
                    pe.wait_ge(aff_ready, 16 + key[1] + 1)
                elif k == "Y":
                    pe.wait_ge(yt_ready, key[1] + 1)
                elif k == "f":
                    pe.wait_ge(yt_ready, 40 + 2 * key[1] + key[2] + 1)
                elif k == "N":
                    l, h = divmod(key[1], 16)
                    pe.wait_ge(decay_ready, HF * l + h + 1)
                elif k == "P":
                    pe.wait_ge(pt_ready, key[1] + 1)
                elif k == "ik":
                    pe.wait_ge(ikt_ready, key[1] + 1)
                elif k == "cum":
                    pe.wait_ge(cum_ready, key[1] + 1)
                elif k == "val":
                    pe.wait_ge(valT_ready, 2 * key[1] + key[2] + 1)
                elif k == "gt":
                    pe.wait_ge(sig_ready, 2 * key[1] + key[2] + 1)
                else:
                    pe.wait_ge(unit_ready, unit_no[key] + 1)

            def t_begin(key):
                n = t_no[key] = len(t_keys)
                if n >= 2:
                    t_released(t_keys[n - 2])
                t_keys.append(key)
                return tb[:, n % 2, :]

            def t_end(ins, key):
                ins.then_inc(t_full[t_no[key] % 2], 1)

            def job_kind(j):
                return "ali" if j >= 32 else "mem" if HF <= j % 16 < HF + HM else "masked"

            def s_begin(key, counted=True):
                if s_keys:
                    k = s_keys[-1]
                    if k[0] == "nar":
                        pe.wait_ge(nar_ready, 2 * k[1] + 1)
                    elif k[0] == "idx":
                        pe.wait_ge(rel_ready, 2 * (6 * k[1] + k[2]) + 1)
                    elif k[0] == "cmean":
                        pe.wait_ge(yc_ready, 1)
                    elif job_kind(k[1]) == "mem":
                        pe.wait_ge(p_ready, k[1] + 1)
                    else:
                        pe.wait_ge(m_ready, k[1] + 1)
                s_keys.append(key)
                if counted:
                    s_no[key] = len(s_no)

            def o_begin(key, counted=True):
                if o_keys:
                    k = o_keys[-1]
                    if k[0] == "nar":
                        pe.wait_ge(nar_ready, 2 * k[1] + 2)
                    elif k[0] == "idx":
                        pe.wait_ge(rel_ready, 2 * (6 * k[1] + k[2]) + 2)
                    elif job_kind(k[1]) == "mem":
                        pe.wait_ge(ym_ready, HM * (k[1] // 16) + k[1] % 16 - HF + 1)
                    else:
                        pe.wait_ge(y_ready, k[2] + 1)
                o_keys.append(key)
                if counted:
                    o_no[key[1] if key[0] == "job" else key] = len(o_no)

            def acc_released(c):
                k = c.name
                if k[0] == "mem" and k[2] == 1:
                    pe.wait_ge(v_ready, k[1] + 1)
                elif k[0] in ("mem", "mq", "mg"):
                    pe.wait_ge(stage_ready, stage_no[(k[0], k[1], 0, 1)] + 1)
                elif k[0] in ("qk", "iq", "dqk"):
                    pe.wait_ge(stage_ready, stage_no[(*k, 1)] + 1)
                elif k[0] in ("vg", "dvg"):
                    d = 6 * k[1] + 3 * (k[0] == "dvg")
                    if k[2] == 0:
                        pe.wait_ge(v_ready, 2 + d + 2)
                    else:
                        pe.wait_ge(g_ready, d + (1 if k[2] == 1 else 3))
                elif k[0] == "o":
                    pe.wait_ge(sum_ready, 4 * k[1] + k[2] + 1)
                elif k[0] in ("val", "gt"):
                    pe.wait_ge(cbuf_ready, 4 * k[1] + 2 * (k[0] == "gt") + 2)
                elif k[0] == "v2":
                    pe.wait_ge(v_ready, 14 + 2 * k[1] + 2)
                elif k[0] == "qk2":
                    pe.wait_ge(cbuf_ready, 8 + 2 * k[1] + 2)
                elif k[0] in ("oa", "ob"):
                    pe.wait_ge(sum_ready, 8 + 4 * (k[0] == "ob") + k[1] + 1)
                elif k[0] == "f1":
                    pe.wait_ge(cbuf_ready, 16 + 2 * (4 * k[1] + k[2]) + 2)
                else:
                    pe.wait_ge(sum_ready, 16 + 4 * k[1] + k[2] + 1)

            acc_users = [c for c in order if c.acc is not None]

            def transpose_unit(key, src, first):
                t = t_begin(key)
                for dt in range(2):
                    for s in range(ST):
                        ins = pe.transpose(t[:, dt * S + s * P:dt * S + s * P + P],
                                           src[:, s, first + dt * P:first + dt * P + P], ident)
                t_end(ins, key)

            def weight_block(g):
                c, i = chunk_at[g]
                w, k = c.width, c.name
                if c.acc is None:
                    outs = [sbank[:, 0:w], obank[:, 0:w]]
                    if i == 0:
                        s_begin(k, counted=False)
                        o_begin(k, counted=False)
                else:
                    outs = [accs(c)[:, s, 0:w] for s in range(ST)]
                    if i == 0 and c.acc >= 2:
                        acc_released(acc_users[c.acc - 2])
                lh, ll = (yh, yl) if k[0] in ("mem", "o", "oa", "ob", "f2") else (xh, xl)
                if k[0] == "mem":
                    pe.wait_ge(xt_ready, i + 1)
                elif k[0] == "nar":
                    pe.wait_ge(xt_ready, 8 + 8 * k[1] + i + 1)
                elif k == ("val", 0):
                    pe.wait_ge(xt_ready, 24 + i + 1)
                elif k[0] == "f1" and k[1] == 0 and k[2] == 0:
                    pe.wait_ge(xt_ready, 32 + i + 1)
                elif k[0] == "o":
                    pe.wait_ge(yt_ready, 16 * k[1] + 2 * i + 2)
                elif k[0] == "oa":
                    pe.wait_ge(yt_ready, 32 + 2 * i + 2)
                elif k[0] == "ob" and i == 0:
                    pe.wait_ge(yt_ready, 32 + H2)
                elif k[0] == "ob":
                    pe.wait_ge(ct_ready, i)
                elif k[0] == "f2":
                    pe.wait_ge(yt_ready, 40 + 8 * k[1] + i + 1)
                pe.wait_ge(low_ready, g + 1)
                n = len(c.rows)
                for t in range(2):
                    kt = c.kts[i] + t
                    hi, lo = high[:, g % RING, t, 0:w], low[:, g % RING, t, 0:w]
                    for s in range(ST):
                        at = slice(s * P, s * P + P)
                        pe.matmul(outs[s], lh[:, kt, at], hi, start=(i == 0 and t == 0), stop=False)
                        pe.matmul(outs[s], ll[:, kt, at], hi, start=False, stop=False)
                        ins = pe.matmul(outs[s], lh[:, kt, at], lo, start=False, stop=(i == n - 1 and t == 1))
                ins.then_inc(block_used, 1)

            def unit_copied(*key):
                pe.wait_ge(unit_ready, unit_no[key] + 1)

            def scores(l, kind, h):
                j = job_no(l, kind, h)
                q, k = (mqT, kmT[l]) if kind == "mem" else (q2T, k2T) if kind == "ali" else (qT, kT)
                if kind == "mem":
                    unit_copied("mem", l, 0, h // 2)
                    unit_copied("mq", l, 0, h // 2)
                elif kind == "ali":
                    unit_copied("qk2", h // 2, 1)
                else:
                    unit_copied("qk" if kind == "fox" else "dqk", l, h // 2, 1)
                if kind == "fox":
                    t = t_begin(("N", j))
                    pe.matmul(t[:, 0:S], logf[:, 0, h:h + 1].broadcast_to([P, P]), upto, start=True, stop=False)
                    ins = pe.matmul(t[:, P:S], logf[:, 1, h:h + 1].broadcast_to([P, P]), tri, start=False, stop=True)
                    t_end(ins, ("N", j))
                s_begin(("job", j))
                if kind == "mem":
                    for s in range(ST):
                        ins = pe.matmul(sbank[:, s * S:s * S + S], q[:, h, s * P:s * P + P], k[:, h, :],
                                        start=True, stop=True)
                else:
                    pe.matmul(sbank[:, 0:P], q[:, h, 0:P], k[:, h, 0:P], start=True, stop=True)
                    ins = pe.matmul(sbank[:, S:2 * S], q[:, h, P:S], k[:, h, :], start=True, stop=True)
                ins.then_inc(s_full, 1)

            def prob_transposes(l, kind, h):
                j = job_no(l, kind, h)
                pe.wait_ge(p_ready, j + 1)
                t = t_begin(("P", j))
                blocks = [(0, 0), (1, 0), (0, 1), (1, 1)] if kind == "mem" else [(0, 0), (1, 0), (1, 1)]
                for n, (s, kk) in enumerate(blocks):
                    ins = pe.transpose(t[:, n * P:n * P + P], sc[:, j % 2, s, kk * P:kk * P + P], ident)
                t_end(ins, ("P", j))

            def values(l, kind, h):
                j = job_no(l, kind, h)
                v = vm[l] if kind == "mem" else v2 if kind == "ali" else vN
                v0, v1 = (v[:, kk, h * HD:h * HD + HD] for kk in range(ST))
                if kind == "mem":
                    pe.wait_ge(v_ready, 2)
                elif kind == "ali":
                    pe.wait_ge(v_ready, 14 + 2 * (h // 4) + 2)
                else:
                    pe.wait_ge(v_ready, 2 + 6 * l + 3 * (kind == "dsa") + h // 2 + 1)
                pe.wait_ge(pt_ready, j + 1)
                o_begin(("job", j, tile_no(l, kind, h)))
                t = pt[:, j % 2, :]
                if kind == "mem":
                    for s in range(ST):
                        o = obank[:, s * P:s * P + P]
                        pe.matmul(o, t[:, s * P:s * P + P], v0, start=True, stop=False)
                        ins = pe.matmul(o, t[:, S + s * P:S + s * P + P], v1, start=False, stop=True)
                else:
                    pe.matmul(obank[:, 0:P], t[:, 0:P], v0, start=True, stop=True)
                    pe.matmul(obank[:, P:S], t[:, P:S], v0, start=True, stop=False)
                    ins = pe.matmul(obank[:, P:S], t[:, S:S + P], v1, start=False, stop=True)
                ins.then_inc(o_full, 1)

            def y_transposes(l, kind, h):
                n = tile_no(l, kind, h)
                pe.wait_ge(y_ready, n + 1)
                t = t_begin(("Y", n))
                src = ymem[:, h] if kind == "mem" else y[:, job_no(l, kind, h) % 2]
                for s in range(ST):
                    ins = pe.transpose(t[:, s * P:s * P + P], src[:, s, :], ident)
                t_end(ins, ("Y", n))

            def attention(l, b, table):
                if b in table:
                    scores(l, *table[b])
                if b - 1 in table:
                    prob_transposes(l, *table[b - 1])
                if b - 2 in table:
                    values(l, *table[b - 2])
                if b - 3 in table and table[b - 3][0] != "mem":
                    y_transposes(l, *table[b - 3])

            def index_scores(l, f):
                s, n, heads = index_shape(f)
                if f == 0:
                    pe.wait_ge(ikt_ready, l + 1)
                    unit_copied("iq", l, 1, 1)
                s_begin(("idx", l, f))
                o_begin(("idx", l, f))
                for e, bank, full in ((0, sbank, s_full), (1, obank, o_full)):
                    part = slice(64 * e, 64 * e + 64)
                    for c, h in enumerate(heads[e::2]):
                        ins = pe.matmul(bank[:, c * n:c * n + n], iqT[part, h // 2, s * P:s * P + P],
                                        ikT[part, 0:n], start=True, stop=True)
                    ins.then_inc(full, 1)

            def staged_unit(*k):
                pe.wait_ge(stage_ready, stage_no[k] + 1)
                transpose_unit(k, stage[stage_no[k] % 2], 0)

            def rotated_unit(*k):
                pe.wait_ge(rot_ready, rot_no[k] + 1)
                transpose_unit(k, rot[rot_no[k] % 2], 0)

            pe.wait_ge(s_in, 32)
            pe.wait_ge(mem_landed, 16)
            for u in range(8):
                transpose_unit(("memT", u), x, 256 * u)
            for b in range(LAYER0):
                weight_block(b)
                i, kb = divmod(b, 8)
                if i in (1, 3) and kb in (2, 3):
                    staged_unit("mem", i // 2, 0, kb - 2)
                if 8 <= b < 24 and b % 2 == 1:
                    pe.wait_ge(x_landed, 16)
                    transpose_unit(("xT", (b - 8) // 2), x, 256 * ((b - 8) // 2))

            for l in range(DEPTH):
                for b in range(LAYER_SLOTS):
                    weight_block(LAYER0 + LAYER_SLOTS * l + b)
                    i, kb, prev = prev_chunk(l, b)
                    if i == 1 and kb == 1:
                        pe.wait_ge(ikr_ready, l + 1)
                        t = t_begin(("ik", l))
                        for s in range(ST):
                            ins = pe.transpose(t[:, s * P:s * P + P], y[:, 0, s, :], ident)
                        t_end(ins, ("ik", l))
                    if i == 1 and kb == 4:
                        pe.wait_ge(logf_ready, l + 1)
                        t = t_begin(("cum", l))
                        pe.matmul(t[:, 0:HF], tri, logf[:, 0, :], start=True, stop=True)
                        pe.matmul(t[:, HF:2 * HF], ones, logf[:, 0, :], start=True, stop=False)
                        ins = pe.matmul(t[:, HF:2 * HF], tri, logf[:, 1, :], start=False, stop=True)
                        t_end(ins, ("cum", l))
                    if i >= 1 and prev[0] == "qk" and kb in (2, 3):
                        staged_unit("qk", l, prev[2], kb - 2)
                    if i >= 1 and prev[0] == "mq" and kb in (2, 3):
                        staged_unit("mq", l, 0, kb - 2)
                    if i >= 1 and prev[0] in ("iq", "dqk") and kb in (3, 4):
                        rotated_unit(prev[0], l, prev[2], kb - 3)
                    if IDX_AT <= b < IDX_AT + 6:
                        index_scores(l, b - IDX_AT)
                    attention(l, b, SCORES)
                    if b in (138, 139):
                        for h in (2 * (b - 138), 2 * (b - 138) + 1):
                            y_transposes(l, "mem", h)
                for u in range(8):
                    pe.wait_ge(norm_ready, 4 * l + u // 2 + 1)
                    transpose_unit(("nT", l, u), x, 256 * u)

            for b in range(BLOCK2_SLOTS):
                weight_block(BLOCK2 + b)
                i, kb = divmod(b, 8)
                if 1 <= i <= 4 and kb in (2, 3):
                    pe.wait_ge(cbuf_ready, 2 * i)
                    transpose_unit((*order[B2 + i - 1].name, kb - 2), chunkbuf[(i - 1) % 2], 256 * (kb - 2))
                if 7 <= i <= 10 and kb in (2, 3):
                    pe.wait_ge(cbuf_ready, 8 + 2 * (i - 7) + 2)
                    transpose_unit(("qk2", i - 7, kb - 2), chunkbuf[(i - 7) % 2], 256 * (kb - 2))
                attention(0, b, SCORES2)
                if b == MEAN_AT:
                    pe.wait_ge(conv_step, CONV_OPS)
                    s_begin(("cmean",))
                    for ct in range(8):
                        ins = pe.matmul(sbank[:, 0:S], ones, cv[:, ct, :], start=(ct == 0), stop=(ct == 7))
                    ins.then_inc(s_full, 1)
                if b == VAR_AT:
                    pe.wait_ge(csq_ready, 1)
                    s_begin(("cvar",))
                    for ct in range(8):
                        ins = pe.matmul(sbank[:, 0:S], ones, hsq[:, ct, :], start=(ct == 0), stop=(ct == 7))
                    ins.then_inc(s_full, 1)
            for u in range(8):
                pe.wait_ge(norm_ready, 8 + u // 2 + 1)
                transpose_unit(("h2T", u), x, 256 * u)

            for q in range(NQ):
                for b in range(FF_SLOTS):
                    weight_block(FF0 + FF_SLOTS * q + b)
                    i, kb = divmod(b, 8)
                    if 1 <= i <= 4 and kb in (2, 3):
                        n = 4 * q + i - 1
                        pe.wait_ge(fsq_ready, n + 1)
                        transpose_unit(("f", n, kb - 2), chunkbuf[n % 2], 256 * (kb - 2))

        @block.scalar
        def _(act):
            def round_block(g):
                c = chunk_at[g][0]
                act.wait_ge(raw_landed[g % RING], landed[g])
                if g >= RING:
                    act.wait_ge(block_used, g - RING + 1)
                act.activation(high[:, g % RING, :, 0:c.width], raw[:, g % RING, :, 0:c.width],
                               ACT.Copy).then_inc(high_ready, 1)

            def unit_high(key, dst):
                t = t_wait(act, key)
                act.activation(flat(dst), t, ACT.Copy).then_inc(hi_ready, 1)

            def acc_done(c):
                act.wait_ge(block_used, c.end)

            def to_stage(c, p, key, func=ACT.Copy):
                n = stage_no[key]
                if p == 0:
                    acc_done(c)
                if n >= 2:
                    old = staged[n - 2]
                    if old in rot_no:
                        act.wait_ge(rot_ready, rot_no[old] + 1)
                    elif old[0] == "mg":
                        act.wait_ge(y_ready, tile_no(old[1], "mem", 2 * old[3] + 1) + 1)
                    else:
                        t_wait(act, old)
                act.activation(stage[n % 2], accs(c)[:, :, 256 * p:256 * p + 256], func).then_inc(stage_ready, 1)

            def unit_out(*key):
                k, l, m, p = key
                if k in ("qk", "dqk"):
                    dst, scale = (qT, kT)[p][:, 2 * m:2 * m + 2, :], (SCALE, 1.0)[p]
                elif k == "mq":
                    dst, scale = mqT[:, 2 * p:2 * p + 2, :], SCALE
                elif k == "iq":
                    dst, scale = iqT[:, 4 * m + 2 * p:4 * m + 2 * p + 2, :], 1.0
                else:
                    dst, scale = kmT[l][:, 2 * p:2 * p + 2, :], 1.0
                t = t_wait(act, key).rearrange("p (a b) -> p a b", a=2)
                act.activation(dst, t, ACT.Copy, scale=scale).then_inc(unit_ready, 1)

            def exps(l, kind, h):
                j = job_no(l, kind, h)
                act.wait_ge(m_ready, j + 1)
                for s in range(ST):
                    n = S if (kind == "mem" or s) else P
                    src = sbank[:, s * S:s * S + n] if kind == "mem" else sc[:, j % 2, s, 0:n]
                    r = 2 * (j % 4) + s
                    ins = act.activation(sc[:, j % 2, s, 0:n], src, ACT.Exp, bias=nmx[:, r:r + 1],
                                         accum_out=rs[:, r:r + 1])
                ins.then_inc(p_ready, 1)

            def prob_copy(l, kind, h):
                j = job_no(l, kind, h)
                t = t_wait(act, ("P", j))
                if j >= 2:
                    act.wait_ge(o_full, o_no[j - 2] + 1)
                n = CW if kind == "mem" else 3 * P
                act.activation(pt[:, j % 2, 0:n], t[:, 0:n], ACT.Copy).then_inc(pt_ready, 1)

            def y_high(n):
                t = t_wait(act, ("Y", n))
                act.activation(yh[:, n % 16, :], t[:, 0:S], ACT.Copy).then_inc(yhi_ready, 1)

            def attention(l, b, table):
                if b in table:
                    exps(l, *table[b])
                if b - 1 in table:
                    prob_copy(l, *table[b - 1])
                if b - 3 in table and table[b - 3][0] != "mem":
                    y_high(tile_no(l, *table[b - 3]))

            def root(n):
                act.wait_ge(var_ready, n)
                act.activation(std, var, ACT.Sqrt).then_inc(std_ready, 1)

            def affine_high(n):
                u = n % 8
                act.wait_ge(aff_ready, n + 1)
                act.activation(flat(xh[:, 2 * u:2 * u + 2, :]), cb[:, u % 4, :], ACT.Copy).then_inc(hi_ready, 1)

            n_sq = [0]

            def squares(src, c):
                for s in range(ST):
                    if n_sq[0]:
                        act.wait_ge(sq_ready, n_sq[0])
                    act.activation(junk, src[:, s, :], ACT.Square, accum_out=ssq[:, s, c:c + 1]).then_inc(sq_ready, 1)
                    n_sq[0] += 1

            for u in range(8):
                unit_high(("memT", u), yh[:, 2 * u:2 * u + 2, :])

            def mem_piece(n, kb):
                l, v = divmod(n, 2)
                c = by[("mem", l, v)]
                if v == 0 and kb in (0, 1):
                    to_stage(c, kb, ("mem", l, 0, kb))
                if v == 0 and kb in (2, 3):
                    unit_out("mem", l, 0, kb - 2)
                if v == 1 and kb == 0:
                    acc_done(c)
                    act.activation(vm[l], accs(c), ACT.Copy).then_inc(v_ready, 1)

            def mem_side(b):
                i, kb = divmod(b, 8)
                if i >= 1:
                    mem_piece(i - 1, kb)
                if 8 <= b < 24 and b % 2 == 1:
                    u = (b - 8) // 2
                    unit_high(("xT", u), xh[:, 2 * u:2 * u + 2, :])

            slots(round_block, mem_side, lambda: mem_piece(3, 0), 0, LAYER0)

            for l in range(DEPTH):
                def layer_side(b, l=l):
                    i, kb, prev = prev_chunk(l, b)
                    if i == 1 and kb == 0:
                        acc_done(by[("nar", l)])
                        act.activation(nar[:, 0, :], sbank[:, 0:NAR], ACT.Copy).then_inc(nar_ready, 1)
                        act.activation(nar[:, 1, :], obank[:, 0:NAR], ACT.Copy).then_inc(nar_ready, 1)
                    if i == 1 and kb == 1:
                        t = t_wait(act, ("ik", l))
                        act.activation(ikT, t[:, 0:S], ACT.Copy).then_inc(ikt_ready, 1)
                        act.wait_ge(flog_in, l + 1)
                        act.activation(fe, fe, ACT.Exp).then_inc(flog_e, 1)
                        act.wait_ge(flog_e, l + 1)
                        act.activation(fl, fe, ACT.Ln, bias=1.0).then_inc(flog_ln, 1)
                    if i >= 1 and prev[0] in ("qk", "iq", "mq", "dqk") and kb in (0, 1):
                        to_stage(by[prev], kb, (prev[0], l, prev[2] if len(prev) > 2 else 0, kb))
                    if i >= 1 and prev[0] in ("qk", "mq") and kb in (2, 3):
                        unit_out(prev[0], l, prev[2] if len(prev) > 2 else 0, kb - 2)
                    if i >= 1 and prev[0] in ("iq", "dqk") and kb in (3, 4):
                        unit_out(prev[0], l, prev[2], kb - 3)
                    if i >= 1 and prev[0] in ("vg", "dvg") and kb in (0, 1):
                        c, part = by[prev], 2 * prev[2] + kb
                        if kb == 0:
                            acc_done(c)
                        if kb == 0 and prev == ("dvg", l, 0):
                            act.wait_ge(o_full, o_no[job_no(l, "fox", HF - 1)] + 1)
                            act.wait_ge(y_ready, tile_no(l, "fox", HF - 1) + 1)
                        src = accs(c)[:, :, 256 * kb:256 * kb + 256]
                        if part < 3:
                            act.activation(vN[:, :, 256 * part:256 * part + 256], src, ACT.Copy).then_inc(v_ready, 1)
                        else:
                            part -= 3
                            act.activation(gN[:, :, 256 * part:256 * part + 256], src, ACT.Silu).then_inc(g_ready, 1)
                    if i >= 1 and prev[0] == "mg" and kb in (0, 1):
                        to_stage(by[prev], kb, ("mg", l, 0, kb), ACT.Silu)
                    if IDX_AT <= b < IDX_AT + 6:
                        f = b - IDX_AT
                        n = 6 * l + f
                        if n >= 2:
                            act.wait_ge(rel_used, n - 1)
                        for e, bank, full, no in ((0, sbank, s_full, s_no), (1, obank, o_full, o_no)):
                            act.wait_ge(full, no[("idx", l, f)] + 1)
                            act.activation(rel[f % 2][e], bank[:, :], ACT.Relu, scale=IDIM ** -0.5).then_inc(rel_ready, 1)
                    attention(l, b, SCORES)
                    if b in (138, 139):
                        for h in (2 * (b - 138), 2 * (b - 138) + 1):
                            y_high(tile_no(l, "mem", h))

                def layer_tail(l=l):
                    root(l + 1)
                    for u in range(8):
                        affine_high(8 * l + u)

                slots(round_block, layer_side, layer_tail, LAYER0 + LAYER_SLOTS * l, LAYER_SLOTS)

            def evac_rows(c, kb, row_scale, func, dst, ready):
                if kb == 0:
                    acc_done(c)
                act.activation(dst, accs(c)[:, kb, :], func, scale=row_scale[:, kb:kb + 1]).then_inc(ready, 1)

            def block2_side(b):
                i, kb = divmod(b, 8)
                c = order[B2 + i - 1]
                k = c.name
                if 2 <= b < 6:
                    act.wait_ge(xres_ready, 4 + b - 2 + 1)
                    squares(x[:, :, CW * (b - 2):CW * (b - 2) + CW], b - 2)
                if b == 6:
                    root(3)
                if 1 <= i <= 4 and kb in (0, 1):
                    if i == 1:
                        act.wait_ge(rs_ready, 1)
                    if i >= 3:
                        t_wait(act, (*order[B2 + i - 3].name, 1))
                    evac_rows(c, kb, rstd2, ACT.Copy, chunkbuf[(i - 1) % 2][:, kb, :], cbuf_ready)
                if 1 <= i <= 4 and kb in (2, 3):
                    m, p = k[1], kb - 2
                    t = t_wait(act, (*k, p))
                    if k[0] == "gt" and m == 1:
                        act.wait_ge(hT_ready, p + 1)
                    for dt in range(2):
                        ct = 4 * m + 2 * p + dt
                        src = t[:, dt * S:dt * S + S]
                        if k[0] == "val":
                            ins = act.activation(hT[:, ct, PAD:PAD + S], src, ACT.Identity, bias=param("bglu", ct))
                        else:
                            ins = act.activation(sc[:, p, dt, :], src, ACT.Sigmoid, bias=param("bglu", 8 + ct))
                    ins.then_inc(valT_ready if k[0] == "val" else sig_ready, 1)
                if i in (5, 6) and kb in (0, 1):
                    evac_rows(c, kb, rstd2, ACT.Copy, v2[:, kb, CW * (i - 5):CW * (i - 5) + CW], v_ready)
                if 7 <= i <= 10 and kb in (0, 1):
                    m = i - 7
                    t_wait(act, ("qk2", m - 2, 1) if m >= 2 else ("val" if m == 0 else "gt", 1, 1))
                    evac_rows(by[("qk2", m)], kb, rstd2, ACT.Copy, chunkbuf[m % 2][:, kb, :], cbuf_ready)
                if 7 <= i <= 10 and kb in (2, 3):
                    m, p = i - 7, kb - 2
                    t = t_wait(act, ("qk2", m, p)).rearrange("p (a b) -> p a b", a=2)
                    act.activation((q2T, k2T)[p][:, 2 * m:2 * m + 2, :], t, ACT.Copy,
                                   scale=(SCALE, 1.0)[p]).then_inc(unit_ready, 1)
                attention(0, b, SCORES2)
                if b == MEAN_AT:
                    act.wait_ge(yc_ready, 1)
                    act.activation(hsq, cv, ACT.Square).then_inc(csq_ready, 1)
                if b == VAR_AT:
                    act.wait_ge(var_ready, 4)
                    act.activation(cstd_b, cvar_b, ACT.Sqrt).then_inc(std_ready, 1)
                if b == VAR_AT + 1:
                    for ct in range(8):
                        act.wait_ge(cn_ready, ct // 2 + 1)
                        act.activation(cv[:, ct, :], cv[:, ct, :], ACT.Silu, bias=param("cb", ct),
                                       scale=param("cg", ct)).then_inc(silu_ready, 1)
                        if ct % 2:
                            act.wait_ge(silu_ready, ct + 1)
                            act.activation(yh[:, 8 + ct - 1:8 + ct + 1, :], cv[:, ct - 1:ct + 1, :],
                                           ACT.Copy).then_inc(ch_ready, 1)
                if b in (98, 103, 108):
                    n = (b - 98) // 5
                    act.wait_ge(sum_ready, 12 + n + 1)
                    squares(mixed[n], n)

            def block2_tail():
                act.wait_ge(sum_ready, 16)
                squares(mixed[3], 3)
                root(5)
                for u in range(8):
                    affine_high(16 + u)
                for c in range(4):
                    act.wait_ge(norm_ready, 8 + c + 1)
                    squares(x[:, :, CW * c:CW * c + CW], c)
                root(6)

            slots(round_block, block2_side, block2_tail, BLOCK2, BLOCK2_SLOTS)

            for q in range(NQ):
                def ff_side(b, q=q):
                    i, kb = divmod(b, 8)
                    n = 4 * q + i - 1
                    if 1 <= i <= 4 and kb in (0, 1):
                        if n >= 2:
                            t_wait(act, ("f", n - 2, 1))
                        else:
                            act.wait_ge(rs_ready, 2)
                        evac_rows(by[("f1", q, i - 1)], kb, rstd3, ACT.Relu, chunkbuf[n % 2][:, kb, :], cbuf_ready)
                    if 1 <= i <= 4 and kb in (2, 3):
                        u = 2 * (i - 1) + kb - 2
                        unit_high(("f", n, kb - 2), yh[:, 2 * u:2 * u + 2, :])
                    if q == NQ - 1 and i >= 5 and kb == 2:
                        act.wait_ge(sum_ready, 28 + i - 5 + 1)
                        squares(mixed[i - 5], i - 5)

                def ff_tail(q=q):
                    if q == NQ - 1:
                        act.wait_ge(sum_ready, 32)
                        squares(mixed[3], 3)
                        root(7)

                slots(round_block, ff_side, ff_tail, FF0 + FF_SLOTS * q, FF_SLOTS)

        @block.vector
        def _(dve):
            n_done = [0]

            def step(ins):
                n_done[0] += 1
                ins.then_inc(dve_done, 1)
                return n_done[0]

            def link(ins):
                dve.wait_ge(dve_done, step(ins))

            def low_block(g):
                c, i = chunk_at[g]
                at = (slice(None), g % RING, slice(None), slice(0, c.width))
                dve.wait_ge(high_ready, g + 1)
                dve.tensor_tensor(low[at], raw[at], high[at].bitcast(F32), ALU.subtract).then_inc(low_ready, 1)

            def unit_low(key, hi, lo, n_hi, ready):
                t = t_wait(dve, key)
                dve.wait_ge(hi_ready, n_hi)
                dve.tensor_tensor(flat(lo), t, flat(hi).bitcast(F32), ALU.subtract).then_inc(ready, 1)

            def rope(l, k, m, p):
                key = (k, l, m, p)
                n, r = stage_no[key], rot_no[key]
                c, s_, d = (icos, isin, IDIM) if k == "iq" else (cos, sin, HD)
                h = 256 // d
                dve.wait_ge(stage_ready, n + 1)
                if r >= 2:
                    t_wait(dve, [q for q in staged if q in rot_no][r - 2])
                v, o, b = (q.rearrange("p s (h d) -> p s h d", d=d) for q in
                           (stage[n % 2], rot[r % 2], rot_b.rearrange("p (s c) -> p s c", s=ST)))
                half = d // 2
                cc = c.unsqueeze(2).broadcast_to([P, ST, h, d])
                ss = s_.unsqueeze(2).broadcast_to([P, ST, h, d])
                step(dve.tensor_tensor(o, v, cc, ALU.mult))
                for s in range(ST):
                    step(dve.tensor_tensor(b[:, s, :, 0:half], v[:, s, :, half:d], ss[:, s, :, 0:half], ALU.mult))
                    last = step(dve.tensor_tensor(b[:, s, :, half:d], v[:, s, :, 0:half], ss[:, s, :, half:d], ALU.mult))
                dve.wait_ge(dve_done, last)
                dve.tensor_tensor(flat(rot[r % 2]), flat(rot[r % 2]), rot_b, ALU.add).then_inc(rot_ready, 1)
                dve.wait_ge(rot_ready, r + 1)

            def newton(v, sd, r, t):
                link(dve.reciprocal(r, sd))
                link(dve.tensor_tensor(t, r, r, ALU.mult))
                link(dve.tensor_tensor(t, t, v, ALU.mult))
                link(dve.tensor_scalar(t, t, -0.5, 1.5, ALU.mult, ALU.add))
                return dve.tensor_tensor(r, r, t, ALU.mult)

            def row_rms(n, n_sq, r):
                dve.wait_ge(sq_ready, n_sq)
                link(dve.tensor_reduce(nt, ssq, AXX, ALU.add))
                dve.tensor_scalar(var, nt, 1.0 / D, RMS_EPS, ALU.mult, ALU.add).then_inc(var_ready, 1)
                dve.wait_ge(std_ready, n)
                return newton(var, std, r, nt)

            def max_of_scores(l, kind, h):
                j = job_no(l, kind, h)
                r = 2 * (j % 4)
                if kind == "fox":
                    t = t_wait(dve, ("N", j))
                    step(dve.scalar_tensor_tensor(out=nfox[:, 0:P], in0=t[:, 0:P], scalar=cum[:, 0, h:h + 1],
                                                  in1=mask[:, 0:P], op0=ALU.subtract, op1=ALU.add))
                    dve.scalar_tensor_tensor(out=nfox[:, P:3 * P], in0=t[:, 0:S], scalar=cum[:, 1, h:h + 1],
                                             in1=mask[:, P:3 * P], op0=ALU.subtract,
                                             op1=ALU.add).then_inc(decay_ready, 1)
                    dve.wait_ge(decay_ready, HF * l + h + 1)
                if kind == "ali":
                    link(dve.tensor_scalar(nfox, dist, 2.0 ** (-8.0 * (h + 1) / H2), None, ALU.mult))
                dve.wait_ge(s_full, s_no[("job", j)] + 1)
                if j >= 2:
                    t_wait(dve, ("P", j - 2))
                if kind == "mem":
                    link(dve.tensor_reduce(mx[:, r:r + 2], sbank[:, :].rearrange("p (s k) -> p s k", s=ST),
                                           AXX, ALU.max))
                else:
                    n0, n1 = (ndsa[:, 0:P], ndsa[:, S:2 * S]) if kind == "dsa" else (nfox[:, 0:P], nfox[:, P:3 * P])
                    step(dve.tensor_tensor_reduce(sc[:, j % 2, 0, 0:P], sbank[:, 0:P], n0, 1.0, -3e38,
                                                  ALU.subtract, ALU.max, mx[:, r:r + 1]))
                    link(dve.tensor_tensor_reduce(sc[:, j % 2, 1, :], sbank[:, S:2 * S], n1, 1.0, -3e38,
                                                  ALU.subtract, ALU.max, mx[:, r + 1:r + 2]))
                dve.tensor_scalar(nmx[:, r:r + 2], mx[:, r:r + 2], -1.0, None, ALU.mult).then_inc(m_ready, 1)

            def outputs(l, kind, h):
                j = job_no(l, kind, h)
                r = 2 * (j % 4)
                dve.wait_ge(p_ready, j + 1)
                link(dve.reciprocal(rinv[:, r:r + 2], rs[:, r:r + 2]))
                dve.wait_ge(o_full, o_no[j] + 1)
                if kind in ("fox", "dsa"):
                    dve.wait_ge(g_ready, 6 * l + 3 * (kind == "dsa") + h // 2 + 1)
                for s in range(ST):
                    o, ri = obank[:, s * P:s * P + P], rinv[:, r + s:r + s + 1]
                    if kind in ("fox", "dsa"):
                        ins = dve.scalar_tensor_tensor(out=y[:, j % 2, s, :], in0=o, scalar=ri,
                                                       in1=gN[:, s, h * HD:h * HD + HD], op0=ALU.mult, op1=ALU.mult)
                    else:
                        dst = ymem[:, h, s, :] if kind == "mem" else y[:, j % 2, s, :]
                        ins = dve.tensor_scalar(dst, o, ri, None, ALU.mult)
                ins.then_inc(ym_ready if kind == "mem" else y_ready, 1)

            def y_low(n):
                t = t_wait(dve, ("Y", n))
                dve.wait_ge(yhi_ready, n + 1)
                dve.tensor_tensor(yl[:, n % 16, :], t[:, 0:S], yh[:, n % 16, :].bitcast(F32),
                                  ALU.subtract).then_inc(yt_ready, 1)

            def attention(l, b, table):
                if b in table:
                    max_of_scores(l, *table[b])
                if b - 2 in table:
                    outputs(l, *table[b - 2])
                if b - 3 in table and table[b - 3][0] != "mem":
                    y_low(tile_no(l, *table[b - 3]))

            def affine(n):
                st, u = divmod(n, 8)
                t = t_wait(dve, ("nT", st, u) if st < 2 else ("h2T", u))
                for dt in range(2):
                    kt = 2 * u + dt
                    dst, src = cb[:, u % 4, dt * S:dt * S + S], t[:, dt * S:dt * S + S]
                    if st == 0:
                        ins = dve.tensor_scalar(dst, src, param("gain", kt), param("bias", kt), ALU.mult, ALU.add)
                    elif st == 1:
                        ins = dve.tensor_scalar(dst, src, gb[:, kt:kt + 1], bb[:, kt:kt + 1], ALU.mult, ALU.add)
                    else:
                        ins = dve.tensor_scalar(dst, src, param("gffn", kt), None, ALU.mult)
                ins.then_inc(aff_ready, 1)

            def affine_low(n):
                u = n % 8
                dve.wait_ge(hi_ready, 16 + n + 1)
                dve.tensor_tensor(flat(xl[:, 2 * u:2 * u + 2, :]), cb[:, u % 4, :],
                                  flat(xh[:, 2 * u:2 * u + 2, :]).bitcast(F32), ALU.subtract).then_inc(xt_ready, 1)

            def affine_units(n0, prepare):
                prepare(0)
                prepare(1)
                for u in range(8):
                    affine(n0 + u)
                    if u % 2 == 0 and u // 2 + 2 < 4:
                        prepare(u // 2 + 2)
                    if u >= 1:
                        affine_low(n0 + u - 1)
                affine_low(n0 + 7)

            dve.wait_ge(s_in, 32)
            g1, b1 = (params[:, PARAM[k][0] + KT:PARAM[k][0] + 2 * KT] for k in ("gain", "bias"))
            gp = params[:, PARAM["gpre"][0]:PARAM["gpre"][1]]
            step(dve.tensor_tensor(gb, g1, gp, ALU.mult))
            link(dve.tensor_tensor(bb, b1, gp, ALU.mult))
            for u in range(8):
                unit_low(("memT", u), yh[:, 2 * u:2 * u + 2, :], yl[:, 2 * u:2 * u + 2, :], u + 1, xt_ready)

            def mem_side(b):
                if 8 <= b < 24 and b % 2 == 1:
                    u = (b - 8) // 2
                    unit_low(("xT", u), xh[:, 2 * u:2 * u + 2, :], xl[:, 2 * u:2 * u + 2, :], 8 + u + 1, xt_ready)

            slots(low_block, mem_side, lambda: None, 0, LAYER0)

            def residual(l, c):
                at = x[:, :, CW * c:CW * c + CW]
                if c == 0:
                    dve.wait_ge(rows_landed, 32 * (l + 1))
                row = [q[:, CW * c:CW * c + CW].unsqueeze(1).broadcast_to([P, ST, CW]) for q in (row_g, row_b)]
                link(dve.tensor_tensor(at, at, row[0], ALU.mult))
                dve.tensor_tensor(at, at, row[1], ALU.add).then_inc(xres_ready, 1)
                dve.wait_ge(xres_ready, 4 * l + c + 1)

            for l in range(DEPTH):
                def add_residual(n, l=l):
                    c = by[("o", l, n)]
                    at = x[:, :, CW * n:CW * n + CW]
                    dve.wait_ge(block_used, c.end)
                    dve.scalar_tensor_tensor(out=at, in0=at, scalar=ALPHA, in1=accs(c), op0=ALU.mult,
                                             op1=ALU.add).then_inc(sum_ready, 1)
                    dve.wait_ge(sum_ready, 4 * l + n + 1)
                    for s in range(ST):
                        last[0] = step(dve.bn_stats(stats[:, s, n, :], x[:, s, CW * n:CW * n + CW]))

                last = [0]

                def layer_side(b, l=l):
                    i, kb, prev = prev_chunk(l, b)
                    if l >= 1 and 1 <= b < 5:
                        residual(l - 1, b - 1)
                    if i == 1 and kb == 0:
                        dve.wait_ge(nar_ready, 2 * l + 2)
                        bf = params[:, PARAM["bf"][0] + HF * l:PARAM["bf"][0] + HF * l + HF]
                        link(dve.tensor_tensor(fz, nar[:, :, IDIM + IH:NAR],
                                               bf.unsqueeze(1).broadcast_to([P, ST, HF]), ALU.add))
                        dve.scalar_tensor_tensor(out=fe, in0=fz, scalar=-1.0, in1=fz, op0=ALU.mult,
                                                 op1=ALU.min).then_inc(flog_in, 1)
                        v, hd = nar[:, :, 0:IDIM], IDIM // 2
                        ta, tb_ = y[:, 1, :, 0:IDIM], y[:, 1, :, IDIM:2 * IDIM]
                        step(dve.tensor_tensor(ta, v, icos, ALU.mult))
                        step(dve.tensor_tensor(tb_[:, :, 0:hd], v[:, :, hd:IDIM], isin[:, :, 0:hd], ALU.mult))
                        link(dve.tensor_tensor(tb_[:, :, hd:IDIM], v[:, :, 0:hd], isin[:, :, hd:IDIM], ALU.mult))
                        dve.tensor_tensor(y[:, 0, :, 0:IDIM], ta, tb_, ALU.add)
                        dve.tensor_tensor(y[:, 0, :, IDIM:2 * IDIM], ta, tb_, ALU.add).then_inc(ikr_ready, 1)
                        step(dve.tensor_scalar(wi, nar[:, :, IDIM:IDIM + IH], IH ** -0.5, None, ALU.mult))
                    if i == 1 and kb == 1:
                        dve.wait_ge(flog_ln, l + 1)
                        dve.scalar_tensor_tensor(out=logf, in0=fz, scalar=0.0, in1=fl, op0=ALU.min,
                                                 op1=ALU.subtract).then_inc(logf_ready, 1)
                    if i == 1 and kb == 4:
                        t = t_wait(dve, ("cum", l))
                        dve.tensor_copy(flat(cum), t[:, 0:2 * HF]).then_inc(cum_ready, 1)
                        dve.wait_ge(cum_ready, l + 1)
                    if i >= 1 and prev[0] in ("iq", "dqk") and kb in (1, 2):
                        rope(l, prev[0], prev[2], kb - 1)
                    if IDX_AT <= b < IDX_AT + 6:
                        index_sum(l, b - IDX_AT)
                    if TOPK_AT <= b < TOPK_AT + TOPK // 8:
                        select_round(b - TOPK_AT)
                    if b == TOPK_AT + TOPK // 8:
                        for s, n in ((0, P), (1, S)):
                            link(dve.tensor_scalar(ndsa[:, s * S:s * S + n], itaken[:, s, 0:n], TAKEN / 1.5, BIG,
                                                   ALU.is_ge, ALU.mult))
                            link(dve.tensor_tensor(ndsa[:, s * S:s * S + n], ndsa[:, s * S:s * S + n],
                                                   mask[:, P * s:P * s + n], ALU.add))
                    attention(l, b, SCORES)
                    if b in (138, 139):
                        for h in (2 * (b - 138), 2 * (b - 138) + 1):
                            n = stage_no[("mg", l, 0, h // 2)]
                            dve.wait_ge(stage_ready, n + 1)
                            dve.wait_ge(ym_ready, HM * l + h + 1)
                            dve.tensor_tensor(ymem[:, h], ymem[:, h], stage[n % 2][:, :, P * (h % 2):P * (h % 2) + P],
                                              ALU.mult).then_inc(y_ready, 1)
                    if b in (139, 140):
                        for h in (2 * (b - 139), 2 * (b - 139) + 1):
                            y_low(tile_no(l, "mem", h))
                    if i >= 18 and kb == 0:
                        add_residual(i - 18)

                def index_sum(l, f):
                    s, n, heads = index_shape(f)
                    if f:
                        dve.wait_ge(rel_used, 6 * l + f)
                    dve.wait_ge(rel_ready, 2 * (6 * l + f) + 2)
                    done = []
                    for c in range(len(heads) // 2):
                        for e, dst in ((0, iscore), (1, itaken)):
                            h = heads[2 * c + e]
                            src, w = rel[f % 2][e][:, c * n:c * n + n], wi[:, s, h:h + 1]
                            if len(done) >= 2:
                                dve.wait_ge(dve_done, done[-2])
                            if h < 2:
                                ins = dve.tensor_scalar(dst[:, s, 0:n], src, w, None, ALU.mult)
                            else:
                                ins = dve.scalar_tensor_tensor(out=dst[:, s, 0:n], in0=src, scalar=w,
                                                               in1=dst[:, s, 0:n], op0=ALU.mult, op1=ALU.add)
                            if c == len(heads) // 2 - 1 and e == 1:
                                ins.then_inc(rel_used, 1)
                            else:
                                done.append(step(ins))
                    dve.wait_ge(dve_done, done[-1])

                def select_round(r, l=l):
                    both = ((0, P), (1, S))
                    if r == 0:
                        dve.wait_ge(rel_used, 6 * l + 6)
                        for s, n in both:
                            step(dve.tensor_tensor(iscore[:, s, 0:n], iscore[:, s, 0:n], itaken[:, s, 0:n], ALU.add))
                        dve.wait_ge(dve_done, n_done[0])
                        for s, n in both:
                            step(dve.tensor_tensor(iscore[:, s, 0:n], iscore[:, s, 0:n], mask[:, P * s:P * s + n],
                                                   ALU.subtract))
                        dve.wait_ge(dve_done, n_done[0])
                    src = iscore if r == 0 else itaken
                    for s, n in both:
                        step(dve.max(top8[:, s, :], src[:, s, 0:n]))
                    dve.wait_ge(dve_done, n_done[0])
                    for s, n in both:
                        step(dve.match_replace(itaken[:, s, 0:n], top8[:, s, :], src[:, s, 0:n], TAKEN))
                    dve.wait_ge(dve_done, n_done[0])

                def layer_tail(l=l):
                    add_residual(3)
                    dve.wait_ge(dve_done, last[0])
                    for s in range(ST):
                        step(dve.bn_aggr(mv[:, s, :], stats[:, s, :, :].rearrange("p c k -> p (c k)")))
                    dve.wait_ge(dve_done, n_done[0])
                    dve.tensor_scalar(var, mv[:, :, 1], LN_EPS, None, ALU.add).then_inc(var_ready, 1)
                    dve.wait_ge(std_ready, l + 1)
                    link(newton(var, std, rstd, nt))

                    def normalise(c):
                        for s in range(ST):
                            at = x[:, s, CW * c:CW * c + CW]
                            ins = dve.tensor_scalar(at, at, mv[:, s, 0:1], rstd[:, s:s + 1], ALU.subtract, ALU.mult)
                        ins.then_inc(norm_ready, 1)

                    affine_units(8 * l, normalise)

                slots(low_block, layer_side, layer_tail, LAYER0 + LAYER_SLOTS * l, LAYER_SLOTS)

            def conv_op(k):
                grp, k2 = divmod(k, 4 * TAPS)
                tap, ct = k2 // 4, 4 * grp + k2 % 4
                src, w = hT[:, ct, tap:tap + S], param("wdw", TAPS * ct + tap)
                if tap == 0:
                    if k2 == 0:
                        dve.wait_ge(hT_ready, 2 * grp + 2)
                    ins = dve.tensor_scalar(cv[:, ct, :], src, w, param("bdw", ct), ALU.mult, ALU.add)
                else:
                    dve.wait_ge(conv_step, k - 3)
                    ins = dve.scalar_tensor_tensor(out=cv[:, ct, :], in0=src, scalar=w, in1=cv[:, ct, :],
                                                   op0=ALU.mult, op1=ALU.add)
                ins.then_inc(conv_step, 1)

            def mix_sum(key, n, count, first):
                c = by[key]
                dve.wait_ge(block_used, c.end)
                if first:
                    ins = dve.tensor_copy(mixed[n], accs(c))
                else:
                    ins = dve.tensor_tensor(mixed[n], mixed[n], accs(c), ALU.add)
                ins.then_inc(sum_ready, 1)
                dve.wait_ge(sum_ready, count)

            def block2_side(b):
                i, kb = divmod(b, 8)
                if b == 0:
                    link(dve.memset(hT[:, :, 0:PAD], 0.0))
                if 1 <= b < 5:
                    residual(1, b - 1)
                if b == 6:
                    row_rms(3, 8, rstd2).then_inc(rs_ready, 1)
                if i in (2, 4) and kb in (2, 3):
                    m, p = i // 2 - 1, kb - 2
                    dve.wait_ge(valT_ready, 2 * m + p + 1)
                    dve.wait_ge(sig_ready, 2 * m + p + 1)
                    at = hT[:, 4 * m + 2 * p:4 * m + 2 * p + 2, PAD:PAD + S]
                    dve.tensor_tensor(at, at, sc[:, p, :, :], ALU.mult).then_inc(hT_ready, 1)
                if b >= CONV_AT:
                    for k in range(CONV_PER_SLOT * (b - CONV_AT), min(CONV_PER_SLOT * (b - CONV_AT + 1), CONV_OPS)):
                        conv_op(k)
                attention(0, b, SCORES2)
                if b in (83, 86, 89, 92):
                    n = (b - 83) // 3
                    mix_sum(("oa", n), n, 8 + n + 1, True)
                if b == MEAN_AT:
                    dve.wait_ge(s_full, s_no[("cmean",)] + 1)
                    dve.scalar_tensor_tensor(out=cv, in0=sbank[:, 0:S].unsqueeze(1).broadcast_to([P, 8, S]),
                                             scalar=-1.0 / CONV, in1=cv, op0=ALU.mult, op1=ALU.add).then_inc(yc_ready, 1)
                if b == VAR_AT:
                    dve.wait_ge(s_full, s_no[("cvar",)] + 1)
                    dve.tensor_scalar(cvar_b, sbank[:, 0:S], 1.0 / CONV, LN_EPS, ALU.mult, ALU.add).then_inc(var_ready, 1)
                    dve.wait_ge(std_ready, 4)
                    link(newton(cvar_b, cstd_b, crs_b, cnt_b))
                    for u in range(4):
                        at = cv[:, 2 * u:2 * u + 2, :]
                        dve.tensor_tensor(at, at, crs_b.unsqueeze(1).broadcast_to([P, 2, S]),
                                          ALU.mult).then_inc(cn_ready, 1)
                if b == VAR_AT + 1:
                    for u in range(4):
                        at = slice(8 + 2 * u, 8 + 2 * u + 2)
                        dve.wait_ge(ch_ready, u + 1)
                        dve.tensor_tensor(yl[:, at, :], cv[:, 2 * u:2 * u + 2, :], yh[:, at, :].bitcast(F32),
                                          ALU.subtract).then_inc(ct_ready, 1)
                if b in (97, 102, 107):
                    n = (b - 97) // 5
                    mix_sum(("ob", n), n, 12 + n + 1, False)

            def add_rows(c, r, row, ready, dst):
                for s in range(ST):
                    step(dve.scalar_tensor_tensor(out=mixed[c][:, s, :], in0=mixed[c][:, s, :], scalar=r[:, s:s + 1],
                                                  in1=row[:, CW * c:CW * c + CW], op0=ALU.mult, op1=ALU.mult))
                dve.wait_ge(dve_done, n_done[0])
                dve.tensor_tensor(dst, x[:, :, CW * c:CW * c + CW], mixed[c], ALU.add).then_inc(ready, 1)

            def block2_tail():
                mix_sum(("ob", 3), 3, 16, False)
                link(row_rms(5, 16, rstdm))
                dve.wait_ge(rows_landed, 80)
                affine_units(16, lambda c: add_rows(c, rstdm, rowp, norm_ready, x[:, :, CW * c:CW * c + CW]))
                row_rms(6, 24, rstd3).then_inc(rs_ready, 1)

            slots(low_block, block2_side, block2_tail, BLOCK2, BLOCK2_SLOTS)

            for q in range(NQ):
                def ff_side(b, q=q):
                    i, kb = divmod(b, 8)
                    n = 4 * q + i - 1
                    if 1 <= i <= 4 and kb == 1:
                        v = chunkbuf[n % 2]
                        dve.wait_ge(cbuf_ready, 16 + 2 * n + 2)
                        dve.tensor_tensor(v, v, v, ALU.mult).then_inc(fsq_ready, 1)
                    if 1 <= i <= 4 and kb in (2, 3):
                        u = 2 * (i - 1) + kb - 2
                        at = slice(2 * u, 2 * u + 2)
                        unit_low(("f", n, kb - 2), yh[:, at, :], yl[:, at, :], 40 + 2 * n + kb - 2 + 1, yt_ready)
                    if i >= 5 and kb == 0:
                        mix_sum(("f2", q, i - 5), i - 5, 16 + 4 * q + i - 5 + 1, q == 0)

                def ff_tail(q=q):
                    mix_sum(("f2", q, 3), 3, 16 + 4 * q + 4, q == 0)
                    if q == NQ - 1:
                        link(row_rms(7, 32, rstd4))
                        dve.wait_ge(rowf_landed, 16)
                        for c in range(4):
                            add_rows(c, rstd4, rowf, fin_ready, mixed[c])

                slots(low_block, ff_side, ff_tail, FF0 + FF_SLOTS * q, FF_SLOTS)

        @block.sync
        def _(sp):
            sp.dma_start(consts[:, :], a["consts"]).then_inc(s_in, 16)
            sp.dma_start(params[:, :], a["params"]).then_inc(s_in, 16)
            sp.dma_start(x[:, :, :], a["mem"][0].rearrange("(s p) d -> p s d", p=P)).then_inc(mem_landed, 16)
            for c in order:
                for i, r0 in enumerate(c.rows):
                    g = c.g0 + i
                    if g >= RING:
                        sp.wait_ge(low_ready, g - RING + 1)
                    rows = c.w[r0:r0 + 2 * P, :].rearrange("(t p) n -> p t n", p=P)
                    dst = raw[:, g % RING, :, :]
                    if c.seg:
                        sp.dma_start(dst[:, :, 0:256], rows[:, :, c.col:c.col + 256]).then_inc(raw_landed[g % RING], 16)
                        k_col = c.col + c.seg
                        sp.dma_start(dst[:, :, 256:512], rows[:, :, k_col:k_col + 256]).then_inc(raw_landed[g % RING], 16)
                    elif c.name[0] == "nar":
                        sp.dma_start(dst[:, :, 0:IDIM + IH], rows[:, :, C_IK:C_IK + IDIM + IH]).then_inc(raw_landed[g % RING], 16)
                        sp.dma_start(dst[:, :, IDIM + IH:NAR], rows[:, :, C_FL:C_FL + HF]).then_inc(raw_landed[g % RING], 16)
                    else:
                        sp.dma_start(dst, rows[:, :, c.col:c.col + CW]).then_inc(raw_landed[g % RING], 16)
            rows_out = out[0].rearrange("(s p) d -> p s d", p=P)
            for c in range(4):
                sp.wait_ge(fin_ready, c + 1)
                sp.dma_start(rows_out[:, :, CW * c:CW * c + CW], mixed[c]).then_inc(out_done, 16)
            sp.wait_ge(out_done, 64)

        @block.gpsimd
        def _(pool):
            t_wait(pool, ("memT", 6))
            t_wait(pool, ("memT", 7))
            pool.dma_start(x[:, :, :], a["x"][0].rearrange("(s p) d -> p s d", p=P)).then_inc(x_landed, 16)
            for l in range(DEPTH):
                pool.wait_ge(block_used, by[("o", l, 3)].end)
                pool.dma_start(row_g, a["ln_gain"][l].partition_broadcast(P)).then_inc(rows_landed, 16)
                pool.dma_start(row_b, a["ln_bias"][l].partition_broadcast(P)).then_inc(rows_landed, 16)
            pool.wait_ge(o_full, o_no[job_no(0, "ali", H2 - 1)] + 1)
            pool.dma_start(rowp, a["g_mix_post_2"][0].partition_broadcast(P)).then_inc(rows_landed, 16)
            pool.wait_ge(ct_ready, 4)
            pool.dma_start(rowf, a["g_ffn_post_2"][0].partition_broadcast(P)).then_inc(rowf_landed, 16)


_WHOLE = ["x", "mem", "w_in", "w_mem_kv", "w_out", "ln_gain", "ln_bias", "w_in_2", "w_out_2", "g_mix_post_2",
          "w_ff1_2", "w_ff2_2", "g_ffn_post_2"]


def tables():
    f = np.float32
    i, j = np.arange(P)[:, None], np.arange(P)[None, :]
    after = (j > i).astype(f)
    out = {"ident": np.eye(P, dtype=f)}
    out["mask"] = np.concatenate([after, np.zeros((P, P), f), after], 1) * f(BIG)
    out["upto"] = np.concatenate([(i <= j).astype(f), np.ones((P, P), f)], 1)
    for name, d in (("", HD), ("i", IDIM)):
        half = d // 2
        freq = f(10000.0) ** (-np.arange(half, dtype=f) / f(half))
        ang = np.arange(S).astype(f)[:, None] * freq[None, :]
        cos, sin = np.cos(ang), np.sin(ang)
        by_part = lambda t: t.reshape(ST, P, d).transpose(1, 0, 2).reshape(P, ST * d)
        out[name + "cos"] = by_part(np.concatenate([cos, cos], 1))
        out[name + "sin"] = by_part(np.concatenate([-sin, sin], 1))
    far = after * f(1e33)
    out["dist"] = np.concatenate([np.abs(i - j) + far, P + i - j, np.abs(i - j) + far], 1)
    return np.ascontiguousarray(np.concatenate([out[k] for k in CONST], 1), dtype=f)


def kernel(**inputs):
    import concourse.bacc as bacc
    from concourse.bass_utils import run_bass_kernel_spmd

    v = {k: np.asarray(a) for k, a in inputs.items()}

    def cols(a):
        return a.reshape(-1, P).T

    parts = {
        "gain": cols(v["ln_gain"]), "bias": cols(v["ln_bias"]), "gpre": cols(v["g_mix_pre_2"]),
        "gffn": cols(v["g_ffn_pre_2"]), "bf": np.broadcast_to(v["b_forget"].reshape(1, -1), (P, DEPTH * HF)),
        "bglu": cols(v["b_glu_2"]), "bdw": cols(v["b_dw_2"]), "cg": cols(v["ln_conv_g_2"]), "cb": cols(v["ln_conv_b_2"]),
        "wdw": v["w_dw_2"][0].reshape(TAPS, 8, P).transpose(2, 1, 0).reshape(P, 8 * TAPS),
    }
    arrays = {k: np.ascontiguousarray(v[k]) for k in _WHOLE}
    arrays["params"] = np.ascontiguousarray(np.concatenate([parts[k] for k in PARAM], 1))
    arrays["consts"] = tables()

    nc = bacc.Bacc("TRN2", target_bir_lowering=False, num_devices=1)
    aps = {k: nc.dram_tensor(f"in_{k}", a.shape, F32, kind="ExternalInput").ap() for k, a in arrays.items()}
    out = nc.dram_tensor("out", v["x"].shape, F32, kind="ExternalOutput").ap()
    build(nc, aps, out)
    r = run_bass_kernel_spmd(nc, [{f"in_{k}": a for k, a in arrays.items()}], core_ids=[0])
    return r.results[0]["out"]
```

```python
from contextlib import ExitStack

import numpy as np

import concourse.bass as bass
from concourse import mybir

F32 = mybir.dt.float32
F32R = mybir.dt.float32r
ACT = mybir.ActivationFunctionType
ALU = mybir.AluOpType
AXX = mybir.AxisListType.X

P = 128
S = 256
ST = S // P
D = 2048
KT = D // P
DEPTH = 2
HD = 128
HF, HS, HM = 6, 6, 4
IH, IDIM = 16, 64
TOPK = min(256, S // 4)
H2 = 8
CONV = 1024
TAPS = 31
PAD = TAPS - 1
CONV_OPS = 8 * TAPS
NQ = 4
ALPHA = (2 * DEPTH) ** 0.25
SCALE = HD ** -0.5
LN_EPS, RMS_EPS = 1e-5, 1e-6
BIG = 1e30
TAKEN = -3e38
RING = 4
LEAD, TURN = 3, 10
CW = 512

C_FQ, C_FK, C_FV, C_FG, C_FL = 0, 768, 1536, 2304, 3072
C_DQ, C_DK, C_DV, C_DG, C_IQ, C_IK = 3078, 3846, 4614, 5382, 6150, 7174
C_MQ, C_MG = 7254, 7766
NAR = IDIM + IH + HF


COLS = [(0, 512), (512, 512), (1024, 256), (1280, 256), (1536, 256), (1792, 256)]
NC = len(COLS)


class Chunk:

    def __init__(self, name, w, col, width, nk, flipped, row0, kt0, n):
        self.name, self.w, self.col, self.width, self.nk, self.flipped = name, w, col, width, nk, flipped
        self.row0, self.kt0, self.n = row0, kt0, n
        self.acc, self.blocks = None, []


def plan(a):
    by, chunk_at, accs = {}, {}, []

    def chunk(key, w, col, width=CW, flipped=False, nk=None, row0=0, kt0=0, kts=KT):
        nk = nk or 2 * CW // width
        c = by[key] = Chunk(key, w, col, width, nk, flipped, row0, kt0, kts // nk)
        if key[0] != "nar":
            c.acc = len(accs)
            accs.append(c)
        return c

    def run(*chunks):
        for i in range(chunks[0].n):
            for c in chunks:
                g = len(chunk_at)
                c.blocks.append(g)
                chunk_at[g] = (c, i)

    def add(key, w, col, **k):
        run(chunk(key, w, col, **k))

    def flip(key, w, col):
        add(key, w, col, width=256, flipped=True)

    for l in range(DEPTH):
        for m in range(2):
            flip(("mk", l, m), a["w_mem_kv"][l], 256 * m)
        add(("mv", l), a["w_mem_kv"][l], HM * HD)
    for l in range(DEPTH):
        w = a["w_in"][l]
        add(("fv", l, 0), w, C_FV)
        add(("nar", l), w, C_IK, width=NAR, nk=8, flipped=True)
        for m in range(2):
            flip(("mg", l, m), w, C_MG + 256 * m)
        for m in range(3):
            flip(("fg", l, m), w, C_FG + 256 * m)
        for m in range(3):
            flip(("fq", l, m), w, C_FQ + 256 * m)
            flip(("fk", l, m), w, C_FK + 256 * m)
        add(("fv", l, 1), w, C_FV + CW, width=256)
        for m in range(2):
            flip(("mq", l, m), w, C_MQ + 256 * m)
        for m in range(4):
            flip(("iq", l, m), w, C_IQ + 256 * m)
        add(("dv", l, 0), w, C_DV)
        for m in range(3):
            flip(("dg", l, m), w, C_DG + 256 * m)
        for m in range(3):
            flip(("dq", l, m), w, C_DQ + 256 * m)
            flip(("dk", l, m), w, C_DK + 256 * m)
        add(("dv", l, 1), w, C_DV + CW, width=256)
        for n, (col, width) in enumerate(COLS):
            add(("o", l, n), a["w_out"][l], col, width=width)
    w = a["w_in_2"][0]
    for m in range(2):
        add(("v2", m), w, 2048 + CW * m)
    for m in range(4):
        flip(("val", m), w, 3072 + 256 * m)
        flip(("gt", m), w, 4096 + 256 * m)
    for m in range(4):
        flip(("q2", m), w, 256 * m)
        flip(("k2", m), w, 1024 + 256 * m)
    w = a["w_out_2"][0]
    for n in range(4):
        add(("oa", n), w, CW * n, kts=6)
    for n, (col, width) in enumerate(COLS):
        add(("ob", n), w, col, width=width, nk=2, row0=768, kt0=6, kts=10)
    for q in range(NQ):
        f1 = [("f1", q, j) for j in range(8)]
        if q == 0:
            run(*[chunk(k, a["w_ff1_2"][0], D * q + 256 * j, width=256, flipped=True) for j, k in enumerate(f1[:2])])
        for j, k in enumerate(f1):
            if q or j >= 2:
                flip(k, a["w_ff1_2"][0], D * q + 256 * j)
        for n, (col, width) in enumerate(COLS):
            add(("f2", q, n), a["w_ff2_2"][0], col, width=width, row0=D * q)
    return by, chunk_at, accs


LAYER_SLOTS, LAYER0 = 162, 32
BLOCK2, BLOCK2_SLOTS = LAYER0 + DEPTH * LAYER_SLOTS, 122
FF0, FF_SLOTS = BLOCK2 + BLOCK2_SLOTS, 64
SCORES = {t: ("fox", h) for h, t in enumerate((40, 42, 48, 50, 56, 58))}
SCORES |= {62 + 2 * h: ("mem", h) for h in range(HM)}
SCORES |= {t: ("dsa", h) for h, t in enumerate((113, 115, 119, 121, 127, 129))}
SCORES2 = {58 + 8 * (h // 2) + 2 * (h % 2): ("ali", h) for h in range(H2)}
IDX_AT, TOPK_AT = 84, 90
CONV_AT, CONV_PER_2_SLOTS = 26, 9
MEAN_AT, VAR_AT, SILU_AT = 85, 88, 90


def job_no(l, kind, h):
    return {"fox": 16 * l + h, "mem": 16 * l + HF + h, "dsa": 16 * l + HM + HF + h, "ali": 32 + h}[kind]


def tile_of(kind, h):
    return {"fox": h, "dsa": HF + h, "mem": HF + HS + h, "ali": h}[kind]


def offsets(sizes):
    at, out = 0, {}
    for name, n in sizes:
        out[name] = (at, at + n)
        at += n
    return out, at


CONST, N_CONST = offsets([("ident", P), ("mask", 3 * P), ("upto", S), ("cos", S), ("sin", S),
                          ("tcos", S), ("tsin", S), ("dist", 3 * P)])
PARAM, N_PARAM = offsets([("gain", DEPTH * KT), ("bias", DEPTH * KT), ("gpre", KT), ("gffn", KT),
                          ("bf", DEPTH * HF), ("bglu", KT), ("bdw", 8), ("cg", 8), ("cb", 8), ("wdw", 8 * TAPS)])


def build(nc, a, out):
    by, chunk_at, acc_users = plan(a)
    with ExitStack() as ctx:
        def sb(name, shape, dt=F32):
            return ctx.enter_context(nc.sbuf_tensor(name, shape, dt))

        def sem(name):
            return ctx.enter_context(nc.semaphore(name))

        raw = sb("raw", [P, RING, 2 * CW])
        high = sb("high", [P, RING, 2 * CW], F32R)
        low = sb("low", [P, RING, 2 * CW], F32R)
        xh = sb("xh", [P, KT, S], F32R)
        xl = sb("xl", [P, KT, S], F32R)
        with nc.sbuf_tensor("yhf", [P, KT, S], F32) as yhf:
            pass
        yh = sb("yh", [P, KT, S], F32R)
        with nc.sbuf_tensor("ylf", [P, KT, S], F32) as ylf:
            pass
        yl = sb("yl", [P, KT, S], F32R)
        x = sb("x_nat", [P, ST, D])
        work = sb("work", [P, 12528])
        cb = sb("cb", [P, 4, CW])
        sc = sb("sc", [P, 2, ST, S])
        pt = sb("pt", [P, 2, CW])
        y = sb("y", [P, 2, S])
        consts = sb("consts", [P, N_CONST])
        params = sb("params", [P, N_PARAM])
        small = sb("small", [P, 384])

        acc = ctx.enter_context(nc.psum_tensor("acc", [P, 4, 512], F32))
        tb = ctx.enter_context(nc.psum_tensor("tb", [P, 2, 512], F32))
        sbank = ctx.enter_context(nc.psum_tensor("sbank", [P, 512], F32))
        obank = ctx.enter_context(nc.psum_tensor("obank", [P, 512], F32))

        def cut(t, at, *dims):
            n = int(np.prod(dims))
            v = t[:, at:at + n]
            if len(dims) == 2:
                v = v.rearrange("p (a b) -> p a b", a=dims[0])
            if len(dims) == 3:
                v = v.rearrange("p (a b c) -> p a b c", a=dims[0], b=dims[1])
            return v

        def flat(v):
            return v.rearrange("p a b -> p (a b)")

        def const(name, *dims):
            return cut(consts, CONST[name][0], *(dims or (CONST[name][1] - CONST[name][0],)))

        def param(name, i, n=1):
            at = PARAM[name][0] + i
            return params[:, at:at + n]

        ident, mask, upto = const("ident"), const("mask"), const("upto")
        tri = upto[:, 0:P]
        ones = upto[:, P:S]
        cos, sin, tcos, tsin = const("cos"), const("sin"), const("tcos"), const("tsin")
        dist = const("dist")

        qT, kT, gT = cut(work, 0, HF, S), cut(work, 1536, HF, S), cut(work, 4608, HF, S)
        vN = cut(work, 3072, ST, 768)
        mqT = cut(work, 6144, HM, S)
        kmT = [cut(work, 7168 + 1024 * l, HM, S) for l in range(DEPTH)]
        vm = [cut(work, 9216 + 1024 * l, ST, 512) for l in range(DEPTH)]
        ikT = cut(work, 11264, S)
        ndsa = cut(work, 11520, 512)
        q2T, k2T, v2 = cut(work, 0, H2, S), cut(work, 2048, H2, S), cut(work, 4096, ST, 1024)
        hT = cut(work, 8192, 8, PAD + S)
        hsq = cut(work, 8192, 8, S)
        cv = cut(work, 10480, 8, S)
        mixed = [cut(work, 6144, ST, CW), cut(work, 7168, ST, CW), cut(work, 0, ST, CW), cut(work, 2048, ST, CW)]

        def mixed_cols(n):
            col, width = COLS[n]
            return mixed[col // CW][:, :, col % CW:col % CW + width]

        rowp, rowf = cut(work, 4096, D), cut(work, 10480, D)
        yhw, ylw = flat(yhf), flat(ylf)
        row_g, row_b = cut(yhw, 0, D), cut(yhw, D, D)
        iscore, itaken = cut(yhw, 6 * S, ST, S), cut(ylw, 6 * S, ST, S)
        iqT = [mqT, cut(yhw, 8 * S, 4, S)]
        nfox = cut(ylw, 8 * S, 3 * P)
        rot_a, rot_b = cb[:, 3, :].rearrange("p (h n) -> p h n", h=2), cut(ylw, 10 * S, 2, S)
        gmT = cut(ylw, 12 * S, HM, S)
        rel = [[cb[:, 2 * f + e, :] for e in range(2)] for f in range(2)]
        junk = pt[:, 0, :]
        gt_b = [cb[:, i, :].rearrange("p (h n) -> p h n", h=2) for i in range(2)]
        rT, rqT = cb[:, 3, 0:S], cb[:, 3, S:2 * S]
        cvar_b, cstd_b, crs_b, cnt_b = cb[:, 0, 0:S], cb[:, 0, S:2 * S], cb[:, 1, 0:S], cb[:, 1, S:2 * S]

        sm = {}
        sm_at = [0]

        def vec(name, n):
            sm[name] = small[:, sm_at[0]:sm_at[0] + n]
            sm_at[0] += n
            assert sm_at[0] <= 384
            return sm[name]

        mx, nmx, rs, rinv = (vec(k, 8) for k in ("mx", "nmx", "rs", "rinv"))
        stats = vec("stats", 96).rearrange("p (s c k) -> p s c k", s=ST, c=8)
        mv = vec("mv", 4).rearrange("p (s k) -> p s k", s=ST)
        var, std, rstd, nt = (vec(k, 2) for k in ("var", "std", "rstd", "nt"))
        rstd2, rstdm, rstd3, rstd4, sq3, nmr = (vec(k, 2) for k in ("rstd2", "rstdm", "rstd3", "rstd4", "sq3", "nmr"))
        ssq = vec("ssq", 2 * NC).rearrange("p (s c) -> p s c", s=ST)
        fz, fe, fl, logf, cum = (vec(k, 12).rearrange("p (s h) -> p s h", s=ST) for k in ("fz", "fe", "fl", "logf", "cum"))
        wi = vec("wi", 32).rearrange("p (s h) -> p s h", s=ST)
        top8 = vec("top8", 16).rearrange("p (s k) -> p s k", s=ST)
        gb, bb = vec("gb", KT), vec("bb", KT)
        warm = vec("warm", 1)

        names = """ident_landed tables_landed rows_landed rowp_landed rowf_landed high_ready low_ready block_used
            s_full o_full m_ready e_ready r_ready p_ready pt_ready y_ready yhi_ready yt_ready kq_ready
            v_ready g_ready rot_ready nar_ready flog_in flog_e flog_ln logf_ready wi_ready warm_done ikt_ready
            cum_ready decay_ready rel_ready rel_used hi_ready xt_ready var_ready std_ready nmr_ready
            norm_ready aff_ready sum_ready sq_ready xres_ready rs_ready rt_ready vg2_ready qk2_ready
            sig_ready vraw_ready hT_ready conv_step low_pool yc_ready csq_ready cn_ready silu_ready ch_ready ct_ready
            relu_ready fsq_ready fin_ready out_done dve_done""".split()
        (ident_landed, tables_landed, rows_landed, rowp_landed, rowf_landed, high_ready,
         low_ready, block_used, s_full, o_full, m_ready, e_ready, r_ready, p_ready, pt_ready, y_ready,
         yhi_ready, yt_ready, kq_ready, v_ready, g_ready, rot_ready, nar_ready, flog_in, flog_e, flog_ln,
         logf_ready, wi_ready, warm_done, ikt_ready, cum_ready, decay_ready, rel_ready, rel_used,
         hi_ready, xt_ready, var_ready, std_ready, nmr_ready, norm_ready, aff_ready, sum_ready, sq_ready,
         xres_ready, rs_ready, rt_ready, vg2_ready, qk2_ready, sig_ready, vraw_ready, hT_ready,
         conv_step, low_pool, yc_ready, csq_ready, cn_ready, silu_ready, ch_ready, ct_ready, relu_ready,
         fsq_ready, fin_ready, out_done, dve_done) = (sem(n) for n in names)
        mem_landed, x_landed = ([sem(f"{n}_landed{i}") for i in range(4)] for n in ("mem", "x"))
        raw_landed = [sem(f"raw_landed{i}") for i in range(RING)]
        t_full = [sem(f"t_full{i}") for i in range(2)]

        t_no, s_no, o_no = {}, {}, {}

        def t_wait(eng, key):
            n = t_no[key]
            eng.wait_ge(t_full[n % 2], n // 2 + 1)
            return tb[:, n % 2, :]

        def accs(c):
            b = 2 * (c.acc % 2)
            return acc[:, b:b + 2, 0:256 if c.width == 256 else CW]

        def part(buf, g):
            c = chunk_at[g][0]
            return buf[:, g % RING, 0:c.nk * c.width].rearrange("p (t n) -> p t n", t=c.nk)

        def slots(block, side, g0, n, done):
            for b in range(done - LEAD):
                side(b)
            for b in range(done, n):
                block(g0 + b)
                if b >= LEAD:
                    side(b - LEAD)

        def last_sides(block, side, g0, n, blocks=LEAD):
            for b in range(n - LEAD, n):
                if b + LEAD < n + blocks:
                    block(g0 + b + LEAD)
                side(b)

        landed = {}
        for g, (c, _) in chunk_at.items():
            landed[g] = landed.get(g - RING, 0) + (32 if c.name[0] == "nar" else 16)

        def keys_out(k):
            if k[0] == "mk":
                return 2 * k[1] + k[2] + 1
            return 4 + 8 * k[1] + {"fq": 1, "fk": 2, "mq": 7}[k[0]] + (1 if k[0] == "mq" else 2) * k[2]

        def gates_out(l, kind, m):
            return 8 * l + {"mem": 0, "fox": 2, "dsa": 5}[kind] + m + 1

        def turned(k):
            return 10 * k[1] + {"iq": 1, "dq": 5, "dk": 6}[k[0]] + (1 if k[0] == "iq" else 2) * k[2]

        def sums(kind, *at):
            return {"o": 0, "oa": 2 * NC, "ob": 2 * NC + 4, "f2": 3 * NC + 4}[kind] + NC * sum(at[:-1]) + at[-1] + 1

        def norms(phase, u):
            return 5 * phase + (u + 1 if u < 2 else 2 + u // 2)

        def values_out(k):
            if k[0] == "mv":
                return k[1] + 1
            return 10 + 2 * k[1] + 2 if k[0] == "v2" else 2 + 4 * k[1] + 2 * (k[0] == "dv") + k[2] + 1

        def ends(b, *kinds):
            c = chunk_at.get(b - 1, (None, 0))[0]
            return c.name if c and c.blocks[-1] == b - 1 and c.name[0] in kinds else None

        def index_shape(f):
            return (0, P, range(8 * f, 8 * f + 8)) if f < 2 else (1, S, range(4 * (f - 2), 4 * (f - 2) + 4))

        pool_blocks = [[LAYER0 + LAYER_SLOTS * l + b for b in range(40, 134) if b % 2] for l in range(DEPTH)]
        pool_blocks.append([BLOCK2 + b for b in range(24, 88) if b % 3])
        by_pool = [g for blocks in pool_blocks for g in blocks]

        def low_taken(eng, g, turn=0):
            if g in by_pool:
                eng.wait_ge(low_pool, by_pool.index(g) + 1)
            else:
                eng.wait_ge(low_ready, FF_SLOTS * turn + g + 1 - sum(p < g for p in by_pool))

        def low_part(eng, g, ready, turn=0):
            eng.wait_ge(high_ready, FF_SLOTS * turn + g + 1)
            eng.tensor_tensor(part(low, g), part(raw, g), part(high, g).bitcast(F32), ALU.subtract).then_inc(ready, 1)

        block = ctx.enter_context(nc.Block())

        @block.tensor
        def _(pe):
            t_keys, s_keys, o_keys = [], [], []

            def t_released(key):
                k = key[0]
                if k == "memT":
                    pe.wait_ge(xt_ready, key[1] + 1)
                elif k == "xT":
                    pe.wait_ge(xt_ready, 8 + key[1] + 1)
                elif k == "nT":
                    pe.wait_ge(aff_ready, 8 * key[1] + key[2] + 1)
                elif k == "h2T":
                    pe.wait_ge(xt_ready, 32 + key[1] + 1)
                elif k == "N":
                    l, h = key[1:]
                    pe.wait_ge(decay_ready, HF * l + h + 1)
                elif k == "P":
                    pe.wait_ge(pt_ready, key[1] + 1)
                elif k == "nar":
                    pe.wait_ge(wi_ready, key[1] + 1)
                elif k == "cum":
                    pe.wait_ge(cum_ready, key[1] + 1)
                else:
                    pe.wait_ge(rt_ready, 1)

            def t_begin(key):
                n = t_no[key] = len(t_keys)
                if n >= 2:
                    t_released(t_keys[n - 2])
                t_keys.append(key)
                return tb[:, n % 2, :]

            def t_end(ins, key):
                ins.then_inc(t_full[t_no[key] % 2], 1)

            def is_mem(j):
                return j < 32 and HF <= j % 16 < HF + HM

            def s_begin(key):
                if s_keys:
                    k = s_keys[-1]
                    if k[0] == "nar":
                        pe.wait_ge(nar_ready, k[1] + 1)
                    elif k[0] == "idx":
                        pe.wait_ge(rel_ready, 2 * (6 * k[1] + k[2]) + 1)
                    elif k[0] == "cmean":
                        pe.wait_ge(yc_ready, 1)
                    elif k[0] == "cvar":
                        pe.wait_ge(var_ready, 4)
                    elif is_mem(k[1]):
                        pe.wait_ge(e_ready, k[1] + 1)
                    else:
                        pe.wait_ge(m_ready, k[1] + 1)
                s_keys.append(key)
                if key[0] != "nar":
                    s_no[key] = len(s_no)

            def o_begin(key):
                if o_keys:
                    k = o_keys[-1]
                    if k[0] == "idx":
                        pe.wait_ge(rel_ready, 2 * (6 * k[1] + k[2]) + 2)
                    elif k[1] >= 32:
                        pe.wait_ge(yt_ready, k[1] + 1)
                    else:
                        pe.wait_ge(y_ready, k[1] + 1)
                o_keys.append(key)
                o_no[key] = len(o_no)

            def acc_released(c, turn):
                k = c.name
                if k[0] == "v2":
                    pe.wait_ge(vraw_ready, k[1] + 1)
                elif k[0] in ("mv", "fv", "dv"):
                    pe.wait_ge(v_ready, values_out(k))
                elif k[0] in ("mk", "fq", "fk", "mq"):
                    pe.wait_ge(kq_ready, keys_out(k))
                elif k[0] in ("mg", "fg", "dg"):
                    pe.wait_ge(g_ready, gates_out(k[1], {"m": "mem", "f": "fox", "d": "dsa"}[k[0][0]], k[2]))
                elif k[0] in ("iq", "dq", "dk"):
                    pe.wait_ge(rot_ready, turned(k))
                elif k[0] == "o":
                    pe.wait_ge(sum_ready, sums(*k))
                elif k[0] in ("val", "gt"):
                    pe.wait_ge(vg2_ready, 2 * k[1] + (k[0] == "gt") + 1)
                elif k[0] in ("q2", "k2"):
                    pe.wait_ge(qk2_ready, 2 * k[1] + (k[0] == "k2") + 1)
                elif k[0] in ("oa", "ob"):
                    pe.wait_ge(sum_ready, sums(*k))
                elif k[0] == "f1":
                    pe.wait_ge(relu_ready, 8 * turn + 8 * k[1] + k[2] + 1)
                else:
                    pe.wait_ge(sum_ready, NC * turn + sums(*k))

            def transpose_unit(key, src, first):
                t = t_begin(key)
                for dt in range(2):
                    for s in range(ST):
                        ins = pe.transpose(t[:, dt * S + s * P:dt * S + s * P + P],
                                           src[:, s, first + dt * P:first + dt * P + P], ident)
                t_end(ins, key)

            def operands_ready(c, i, turn):
                k, first = c.name, c.nk * i // 2 + c.nk // 2
                if k[0] in ("mk", "mv"):
                    pe.wait_ge(xt_ready, first)
                elif k[0] == "fv" and k[2] == 0:
                    pe.wait_ge(xt_ready, 8 + 8 * k[1] + first)
                elif k == ("v2", 0):
                    pe.wait_ge(xt_ready, 24 + first)
                elif k in (("f1", 0, 0), ("f1", 0, 1)):
                    pe.wait_ge(xt_ready, 32 + first)
                elif k[0] in ("o", "oa", "ob", "f2") and k[-1]:
                    pass
                elif k[0] == "o" and i < 6:
                    pe.wait_ge(yt_ready, 16 * k[1] + HF + HM + (2 * i - 4 if i >= 3 else 0))
                elif k[0] == "oa":
                    pe.wait_ge(yt_ready, 32 + 2 * i + 2)
                elif k[0] == "ob" and i == 0:
                    pe.wait_ge(yt_ready, 32 + H2)
                elif k[0] == "ob":
                    pe.wait_ge(ct_ready, i)
                elif k[0] == "f2":
                    pe.wait_ge(yt_ready, 8 * turn + 40 + 8 * k[1] + i + 1)

            def weight_block(g, turn=0):
                c, i = chunk_at[g]
                k = c.name
                if k[0] == "nar":
                    outs = [sbank[0:NAR, 0:S]]
                    if i == 0:
                        s_begin(k)
                else:
                    outs = [accs(c)[:, s, :] for s in range(2)]
                    if i == 0 and c.acc >= 2:
                        acc_released(acc_users[c.acc - 2], turn)
                vh, vl = (yh, yl) if k[0] in ("mk", "mv", "o", "oa", "ob", "f2") else (xh, xl)
                operands_ready(c, i, turn)
                low_taken(pe, g, turn)
                wh, wl = part(high, g), part(low, g)
                for t in range(c.nk):
                    kt = c.kt0 + c.nk * i + t
                    first, last = i == 0 and t == 0, i == c.n - 1 and t == c.nk - 1
                    for s in range(len(outs)):
                        at = slice(s * P, min(s * P + P, c.width if c.flipped else S))
                        if c.flipped:
                            products = ((wh[:, t, at], vh[:, kt, :]), (wh[:, t, at], vl[:, kt, :]),
                                        (wl[:, t, at], vh[:, kt, :]))
                        else:
                            products = ((vh[:, kt, at], wh[:, t, :]), (vh[:, kt, at], wl[:, t, :]),
                                        (vl[:, kt, at], wh[:, t, :]))
                        for n, (stationary, moving) in enumerate(products):
                            ins = pe.matmul(outs[s], stationary, moving, start=first and n == 0, stop=last and n == 2)
                ins.then_inc(block_used, 1)

            def scores(l, kind, h):
                j = job_no(l, kind, h)
                q, k = (mqT, kmT[l]) if kind == "mem" else (q2T, k2T) if kind == "ali" else (qT, kT)
                if kind == "mem":
                    pe.wait_ge(kq_ready, keys_out(("mq", l, h // 2)))
                elif kind == "ali":
                    pe.wait_ge(qk2_ready, 2 * (h // 2) + 2)
                elif kind == "fox":
                    pe.wait_ge(kq_ready, keys_out(("fk", l, h // 2)))
                else:
                    pe.wait_ge(rot_ready, turned(("dk", l, h // 2)))
                if kind == "fox":
                    t = t_begin(("N", l, h))
                    pe.matmul(t[:, 0:S], logf[:, 0, h:h + 1].broadcast_to([P, P]), upto, start=True, stop=False)
                    ins = pe.matmul(t[:, P:S], logf[:, 1, h:h + 1].broadcast_to([P, P]), tri, start=False, stop=True)
                    t_end(ins, ("N", l, h))
                s_begin(("job", j))
                if kind == "mem":
                    for s in range(ST):
                        ins = pe.matmul(sbank[:, s * S:s * S + S], q[:, h, s * P:s * P + P], k[:, h, :],
                                        start=True, stop=True)
                else:
                    pe.matmul(sbank[:, 0:P], q[:, h, 0:P], k[:, h, 0:P], start=True, stop=True)
                    ins = pe.matmul(sbank[:, S:2 * S], q[:, h, P:S], k[:, h, :], start=True, stop=True)
                ins.then_inc(s_full, 1)

            def prob_transposes(l, kind, h):
                j = job_no(l, kind, h)
                pe.wait_ge(p_ready, j + 1)
                t = t_begin(("P", j))
                blocks = [(0, 0), (1, 0), (0, 1), (1, 1)] if kind == "mem" else [(0, 0), (1, 0), (1, 1)]
                for n, (s, kk) in enumerate(blocks):
                    ins = pe.transpose(t[:, n * P:n * P + P], sc[:, j % 2, s, kk * P:kk * P + P], ident)
                t_end(ins, ("P", j))

            def values(l, kind, h):
                j = job_no(l, kind, h)
                v = vm[l] if kind == "mem" else v2 if kind == "ali" else vN
                v0, v1 = (v[:, kk, h * HD:h * HD + HD] for kk in range(ST))
                if kind == "mem":
                    pe.wait_ge(v_ready, values_out(("mv", l)))
                elif kind == "ali":
                    pe.wait_ge(v_ready, values_out(("v2", h // 4)))
                else:
                    pe.wait_ge(v_ready, values_out((kind[0] + "v", l, h // 4)))
                pe.wait_ge(pt_ready, j + 1)
                o_begin(("job", j))
                t = pt[:, j % 2, :]
                if kind == "mem":
                    pe.matmul(obank[:, 0:S], v0, t[:, 0:S], start=True, stop=False)
                    ins = pe.matmul(obank[:, 0:S], v1, t[:, S:2 * S], start=False, stop=True)
                else:
                    pe.matmul(obank[:, 0:S], v0, t[:, 0:S], start=True, stop=False)
                    ins = pe.matmul(obank[:, P:S], v1, t[:, S:S + P], start=False, stop=True)
                ins.then_inc(o_full, 1)

            def attention(l, b, table):
                if b - 3 in table:
                    values(l, *table[b - 3])
                if b - 2 in table:
                    prob_transposes(l, *table[b - 2])
                if b in table:
                    scores(l, *table[b])

            def index_scores(l, f):
                s, n, heads = index_shape(f)
                if f == 0:
                    pe.wait_ge(ikt_ready, l + 1)
                    pe.wait_ge(rot_ready, turned(("iq", l, 3)))
                s_begin(("idx", l, f))
                o_begin(("idx", l, f))
                for e, bank, full in ((0, sbank, s_full), (1, obank, o_full)):
                    half = slice(64 * e, 64 * e + 64)
                    for c, h in enumerate(heads[e::2]):
                        q = iqT[h // 8][half, h // 2 % 4, s * P:s * P + P]
                        ins = pe.matmul(bank[:, c * n:c * n + n], q, ikT[half, 0:n], start=True, stop=True)
                    ins.then_inc(full, 1)

            def mem_unit(u):
                pe.wait_ge(mem_landed[u // 2], 16)
                transpose_unit(("memT", u), x, 256 * u)

            pe.wait_ge(ident_landed, 16)
            mem_unit(0)
            mem_unit(1)
            for b in range(LAYER0):
                for u in (2 * b + 2, 2 * b + 3):
                    if u < 8:
                        mem_unit(u)
                weight_block(b)
                if 8 <= b < 24 and b % 2 == 1:
                    u = (b - 8) // 2
                    pe.wait_ge(x_landed[u // 2], 16)
                    transpose_unit(("xT", u), x, 256 * u)
            pe.wait_ge(tables_landed, 32)

            for l in range(DEPTH):
                g0 = LAYER0 + LAYER_SLOTS * l
                for b in range(LAYER_SLOTS):
                    if l and b < 6:
                        pe.wait_ge(norm_ready, norms(l - 1, b + 2))
                        transpose_unit(("nT", l - 1, b + 2), x, 256 * (b + 2))
                    weight_block(g0 + b)
                    if b == 11:
                        pe.wait_ge(nar_ready, l + 1)
                        t = t_begin(("nar", l))
                        for s in range(ST):
                            ins = pe.transpose(t[:, s * P:s * P + NAR], y[0:NAR, 1, s * P:s * P + P],
                                               ident[0:NAR, 0:NAR])
                        t_end(ins, ("nar", l))
                    if b == 15:
                        pe.wait_ge(logf_ready, l + 1)
                        t = t_begin(("cum", l))
                        pe.matmul(t[:, 0:HF], tri, logf[:, 0, :], start=True, stop=True)
                        pe.matmul(t[:, HF:2 * HF], ones, logf[:, 0, :], start=True, stop=False)
                        ins = pe.matmul(t[:, HF:2 * HF], tri, logf[:, 1, :], start=False, stop=True)
                        t_end(ins, ("cum", l))
                    if IDX_AT <= b < IDX_AT + 6:
                        index_scores(l, b - IDX_AT)
                    attention(l, b, SCORES)
                for u in range(2):
                    pe.wait_ge(norm_ready, norms(l, u))
                    transpose_unit(("nT", l, u), x, 256 * u)

            for b in range(BLOCK2_SLOTS):
                if b < 6:
                    pe.wait_ge(norm_ready, norms(1, b + 2))
                    transpose_unit(("nT", 1, b + 2), x, 256 * (b + 2))
                weight_block(BLOCK2 + b)
                if b == 18:
                    pe.wait_ge(rs_ready, 1)
                    t = t_begin(("rT",))
                    for s in range(ST):
                        ins = pe.matmul(t[:, s * P:s * P + P], rstd2[:, s:s + 1].broadcast_to([P, P]), ident,
                                        start=True, stop=True)
                    t_end(ins, ("rT",))
                attention(0, b, SCORES2)
                if b == MEAN_AT:
                    pe.wait_ge(conv_step, CONV_OPS)
                    s_begin(("cmean",))
                    for ct in range(8):
                        ins = pe.matmul(sbank[:, 0:S], ones, cv[:, ct, :], start=(ct == 0), stop=(ct == 7))
                    ins.then_inc(s_full, 1)
                if b == VAR_AT:
                    pe.wait_ge(csq_ready, 1)
                    s_begin(("cvar",))
                    for ct in range(8):
                        ins = pe.matmul(sbank[:, 0:S], ones, hsq[:, ct, :], start=(ct == 0), stop=(ct == 7))
                    ins.then_inc(s_full, 1)
            for u in range(2):
                pe.wait_ge(norm_ready, norms(2, u))
                transpose_unit(("h2T", u), x, 256 * u)
            for b in range(FF_SLOTS):
                for u in {1: (2, 3), 2: (4,), 3: (5,), 4: (6,), 5: (7,)}.get(b, ()):
                    pe.wait_ge(norm_ready, norms(2, u))
                    transpose_unit(("h2T", u), x, 256 * u)
                weight_block(FF0 + b)
            with pe.Fori(0, NQ - 1) as turn:
                for b in range(FF_SLOTS):
                    weight_block(FF0 + FF_SLOTS + b, turn)

        @block.scalar
        def _(act):
            def round_block(g, turn=0):
                act.wait_ge(raw_landed[g % RING], 16 * FF_SLOTS // RING * turn + landed[g])
                if g >= RING:
                    act.wait_ge(block_used, FF_SLOTS * turn + g - RING + 1)
                act.activation(part(high, g), part(raw, g), ACT.Copy).then_inc(high_ready, 1)

            def unit_high(key, dst):
                t = t_wait(act, key)
                act.activation(flat(dst), t, ACT.Copy).then_inc(hi_ready, 1)

            def acc_done(c, turn=0):
                act.wait_ge(block_used, FF_SLOTS * turn + c.blocks[-1] + 1)

            def exps(l, kind, h):
                j = job_no(l, kind, h)
                act.wait_ge(m_ready, j + 1)
                if kind == "mem" and j >= 2:
                    t_wait(act, ("P", j - 2))
                for s in range(ST):
                    n = S if (kind == "mem" or s) else P
                    src = sbank[:, s * S:s * S + n] if kind == "mem" else sc[:, j % 2, s, 0:n]
                    r = 2 * (j % 4) + s
                    ins = act.activation(sc[:, j % 2, s, 0:n], src, ACT.Exp, bias=nmx[:, r:r + 1],
                                         accum_out=rs[:, r:r + 1])
                ins.then_inc(e_ready, 1)

            def probs(l, kind, h):
                j = job_no(l, kind, h)
                act.wait_ge(r_ready, j + 1)
                for s in range(ST):
                    n = S if (kind == "mem" or s) else P
                    r = 2 * (j % 4) + s
                    ins = act.activation(sc[:, j % 2, s, 0:n], sc[:, j % 2, s, 0:n], ACT.Copy, scale=rinv[:, r:r + 1])
                ins.then_inc(p_ready, 1)

            def prob_copy(l, kind, h):
                j = job_no(l, kind, h)
                t = t_wait(act, ("P", j))
                if j >= 2:
                    act.wait_ge(o_full, o_no[("job", j - 2)] + 1)
                n = CW if kind == "mem" else 3 * P
                act.activation(pt[:, j % 2, 0:n], t[:, 0:n], ACT.Copy).then_inc(pt_ready, 1)

            def y_high(l, kind, h):
                j = job_no(l, kind, h)
                if kind == "ali":
                    act.wait_ge(o_full, o_no[("job", j)] + 1)
                    src = obank[:, 0:S]
                else:
                    act.wait_ge(y_ready, j + 1)
                    src = y[:, j % 2, :]
                act.activation(yh[:, tile_of(kind, h), :], src, ACT.Copy).then_inc(yhi_ready, 1)

            def attention(l, b, table):
                if b - 2 in table:
                    prob_copy(l, *table[b - 2])
                if b - 4 in table:
                    y_high(l, *table[b - 4])
                if b - 1 in table:
                    probs(l, *table[b - 1])
                if b in table:
                    exps(l, *table[b])

            n_ahead = [0]

            def root_ahead():
                n_ahead[0] += 1
                act.activation(warm, ident[:, 0:1], ACT.Sqrt).then_inc(warm_done, 1)
                act.wait_ge(warm_done, n_ahead[0])

            def root(n):
                act.wait_ge(var_ready, n)
                act.activation(std, var, ACT.Sqrt).then_inc(std_ready, 1)

            n_sq = [0]

            def squares(src, c):
                for s in range(ST):
                    if n_sq[0]:
                        act.wait_ge(sq_ready, n_sq[0])
                    act.activation(junk[:, 0:src.shape[-1]], src[:, s, :], ACT.Square, accum_out=ssq[:, s, c:c + 1]).then_inc(sq_ready, 1)
                    n_sq[0] += 1

            def copied_out(name):
                c = by[name]
                k, l = name[0:2]
                acc_done(c)
                if k == "mv":
                    act.activation(vm[l], accs(c), ACT.Copy).then_inc(v_ready, 1)
                elif k in ("fv", "dv"):
                    if name == ("dv", l, 0):
                        act.wait_ge(o_full, o_no[("job", job_no(l, "fox", HF - 1))] + 1)
                    at = CW * name[2]
                    act.activation(vN[:, :, at:at + c.width], accs(c), ACT.Copy).then_inc(v_ready, 1)
                elif k in ("mk", "fq", "fk", "mq"):
                    dst = {"mk": kmT[l], "fq": qT, "fk": kT, "mq": mqT}[k][:, 2 * name[2]:2 * name[2] + 2, :]
                    scale = SCALE if k in ("fq", "mq") else 1.0
                    act.activation(dst, accs(c), ACT.Copy, scale=scale).then_inc(kq_ready, 1)
                else:
                    if k == "dg":
                        act.wait_ge(y_ready, job_no(l, "fox", HF - 1) + 1)
                    dst = (gmT if k == "mg" else gT)[:, 2 * name[2]:2 * name[2] + 2, :]
                    act.activation(dst, accs(c), ACT.Silu).then_inc(g_ready, 1)

            for u in range(8):
                unit_high(("memT", u), yh[:, 2 * u:2 * u + 2, :])
                if u % 2:
                    round_block(u // 2)

            def mem_side(b):
                name = ends(b, "mk", "mv")
                if name:
                    copied_out(name)
                if 8 <= b < 24 and b % 2 == 1:
                    u = (b - 8) // 2
                    unit_high(("xT", u), xh[:, 2 * u:2 * u + 2, :])

            slots(round_block, mem_side, 0, LAYER0, 4)
            last_sides(round_block, mem_side, 0, LAYER0)
            act.wait_ge(tables_landed, 32)

            for l in range(DEPTH):
                g0 = LAYER0 + LAYER_SLOTS * l

                def layer_side(b, l=l, g0=g0):
                    name = ends(g0 + b, "mv", "fq", "fk", "mq", "fv", "dv", "mg", "fg", "dg")
                    if name:
                        copied_out(name)
                    if b == 10:
                        act.wait_ge(block_used, by[("nar", l)].blocks[-1] + 1)
                        act.activation(y[0:NAR, 1, :], sbank[0:NAR, 0:S], ACT.Copy).then_inc(nar_ready, 1)
                    if b == 11:
                        act.wait_ge(flog_in, l + 1)
                        act.activation(fe, fe, ACT.Exp).then_inc(flog_e, 1)
                        act.wait_ge(flog_e, l + 1)
                        act.activation(fl, fe, ACT.Ln, bias=1.0).then_inc(flog_ln, 1)
                    if b == 150:
                        root_ahead()
                    if IDX_AT <= b < IDX_AT + 6:
                        f = b - IDX_AT
                        n = 6 * l + f
                        if n >= 2:
                            act.wait_ge(rel_used, n - 1)
                        for e, bank, full, no in ((0, sbank, s_full, s_no), (1, obank, o_full, o_no)):
                            act.wait_ge(full, no[("idx", l, f)] + 1)
                            act.activation(rel[f % 2][e], bank[:, :], ACT.Relu, scale=IDIM ** -0.5).then_inc(rel_ready, 1)
                    attention(l, b, SCORES)

                def normalise(u, n=1):
                    for s in range(ST):
                        at = x[:, s, 256 * u:256 * (u + n)]
                        ins = act.activation(at, at, ACT.Identity, bias=nmr[:, s:s + 1], scale=rstd[:, s:s + 1])
                    ins.then_inc(norm_ready, 1)

                def affine_high(n):
                    u = n % 8
                    act.wait_ge(aff_ready, n + 1)
                    act.activation(flat(xh[:, 2 * u:2 * u + 2, :]), cb[:, u % 4, :], ACT.Copy).then_inc(hi_ready, 1)

                slots(round_block, layer_side, g0, LAYER_SLOTS, TURN if l else LEAD)
                last_sides(round_block, layer_side, g0, LAYER_SLOTS)
                nxt = g0 + LAYER_SLOTS
                root(l + 1)
                round_block(nxt + 3)
                act.wait_ge(nmr_ready, l + 1)
                normalise(0)
                normalise(1)
                normalise(2, 2)
                for u in range(8):
                    affine_high(8 * l + u)
                    if u in (0, 2):
                        normalise(u + 4, 2)
                    if u >= 2:
                        round_block(nxt + 2 + u)

            def block2_side(b):
                name = ends(BLOCK2 + b, "val", "gt", "v2")
                if b in (8, 10, 12, 14):
                    c = (b - 8) // 2
                    act.wait_ge(xres_ready, 4 + c + 1)
                    squares(x[:, :, CW * c:CW * c + CW], c)
                if b == 16:
                    root(3)
                if name and name[0] == "v2":
                    m = name[1]
                    acc_done(by[name])
                    act.activation(v2[:, :, CW * m:CW * m + CW], accs(by[name]), ACT.Copy).then_inc(vraw_ready, 1)
                if b in (19, 20):
                    if b == 19:
                        act.wait_ge(rs_ready, 1)
                        act.wait_ge(vraw_ready, 2)
                    for s in range(ST):
                        v = v2[:, s, CW * (b - 19):CW * (b - 19) + CW]
                        act.activation(v, v, ACT.Copy, scale=rstd2[:, s:s + 1]).then_inc(v_ready, 1)
                if name and name[0] == "gt":
                    m = name[1]
                    act.wait_ge(vg2_ready, 2 * m + 2)
                    for i in range(2):
                        v = gt_b[m % 2][:, i, :]
                        ins = act.activation(v, v, ACT.Sigmoid, bias=param("bglu", 8 + 2 * m + i))
                    ins.then_inc(sig_ready, 1)
                attention(0, b, SCORES2)
                if b == MEAN_AT:
                    act.wait_ge(yc_ready, 1)
                    act.activation(hsq, cv, ACT.Square).then_inc(csq_ready, 1)
                if b == VAR_AT:
                    act.wait_ge(var_ready, 4)
                    act.activation(cstd_b, cvar_b, ACT.Sqrt).then_inc(std_ready, 1)
                if SILU_AT <= b < SILU_AT + 4:
                    u = b - SILU_AT
                    act.wait_ge(cn_ready, u + 1)
                    for ct in (2 * u, 2 * u + 1):
                        act.activation(cv[:, ct, :], cv[:, ct, :], ACT.Silu, bias=param("cb", ct),
                                       scale=param("cg", ct)).then_inc(silu_ready, 1)
                    act.wait_ge(silu_ready, 2 * u + 2)
                    act.activation(yh[:, 8 + 2 * u:8 + 2 * u + 2, :], cv[:, 2 * u:2 * u + 2, :],
                                   ACT.Copy).then_inc(ch_ready, 1)
                if b == 96:
                    root_ahead()
                if b in (98, 103, 108, 113, 118):
                    n = (b - 98) // 5
                    act.wait_ge(sum_ready, sums("ob", n))
                    squares(mixed_cols(n), n)

            slots(round_block, block2_side, BLOCK2, BLOCK2_SLOTS, TURN)
            last_sides(round_block, block2_side, BLOCK2, BLOCK2_SLOTS)
            act.wait_ge(sum_ready, sums("ob", NC - 1))
            squares(mixed_cols(NC - 1), NC - 1)
            root(5)
            round_block(FF0 + 3)
            for u in range(8):
                t = t_wait(act, ("h2T", u))
                for dt in range(2):
                    kt = 2 * u + dt
                    ins = act.activation(xh[:, kt, :], t[:, dt * S:dt * S + S], ACT.Copy, scale=param("gffn", kt))
                ins.then_inc(hi_ready, 1)
                if u >= 2:
                    round_block(FF0 + 2 + u)

            def relu_square(name, turn):
                c = by[name]
                n, j = 8 * name[1] + name[2], name[2]
                f = cb[:, j % 4, :]
                if n >= 4:
                    act.wait_ge(yt_ready, 8 * turn + 40 + n - 4 + 1)
                acc_done(c, turn)
                act.activation(f.rearrange("p (h n) -> p h n", h=2), accs(c), ACT.Relu).then_inc(relu_ready, 1)
                act.wait_ge(relu_ready, 8 * turn + n + 1)
                act.activation(f, f, ACT.Square).then_inc(fsq_ready, 1)
                act.wait_ge(fsq_ready, 8 * turn + n + 1)
                act.activation(flat(yh[:, 2 * j:2 * j + 2, :]), f, ACT.Copy).then_inc(yhi_ready, 1)

            def ff_side(b, q, turn=0):
                name = ends(FF0 + FF_SLOTS * q + b, "f1")
                if q == 0 and b in (10, 12, 14, 16):
                    c = (b - 10) // 2
                    act.wait_ge(norm_ready, norms(2, 2 * c + 1))
                    squares(x[:, :, CW * c:CW * c + CW], c)
                if q == 0 and b == 18:
                    root(6)
                if name:
                    relu_square(name, turn)

            slots(round_block, lambda b: ff_side(b, 0), FF0, FF_SLOTS, TURN)
            with act.Fori(0, NQ - 1) as turn:
                slots(lambda g: round_block(g, turn), lambda b: ff_side(b, 1, turn), FF0 + FF_SLOTS, FF_SLOTS, 0)
            for n in range(NC):
                act.wait_ge(sum_ready, sums("f2", NQ - 1, n))
                squares(mixed_cols(n), n)
            root(7)

        @block.vector
        def _(dve):
            n_done = [0]

            def step(ins):
                n_done[0] += 1
                ins.then_inc(dve_done, 1)
                return n_done[0]

            def link(ins):
                dve.wait_ge(dve_done, step(ins))

            def acc_done(c, turn=0):
                dve.wait_ge(block_used, FF_SLOTS * turn + c.blocks[-1] + 1)

            def low_block(g, turn=0):
                if g not in by_pool:
                    low_part(dve, g, low_ready, turn)

            def unit_low(key, hi, lo, n_hi):
                t = t_wait(dve, key)
                dve.wait_ge(hi_ready, n_hi)
                dve.tensor_tensor(flat(lo), t, flat(hi).bitcast(F32), ALU.subtract).then_inc(xt_ready, 1)

            def rope(k):
                c, n = by[k], turned(k)
                cs, sn, half = (tcos, tsin, IDIM // 2) if k[0] == "iq" else (cos, sin, HD // 2)
                if k[0] == "iq":
                    dst = iqT[k[2] // 2][:, 2 * (k[2] % 2):2 * (k[2] % 2) + 2, :]
                else:
                    dst = (qT if k[0] == "dq" else kT)[:, 2 * k[2]:2 * k[2] + 2, :]
                acc_done(c)
                v = accs(c)
                step(dve.tensor_tensor(rot_a, v, cs.unsqueeze(1).broadcast_to([P, 2, S]), ALU.mult))
                for p0 in range(0, P, half):
                    p1 = p0 + half if p0 // half % 2 == 0 else p0 - half
                    last = step(dve.tensor_tensor(rot_b[p0:p0 + half], v[p1:p1 + half],
                                                  sn[p1:p1 + half].unsqueeze(1).broadcast_to([half, 2, S]), ALU.mult))
                dve.wait_ge(dve_done, last)
                dve.tensor_tensor(dst, rot_a, rot_b, ALU.add).then_inc(rot_ready, 1)
                dve.wait_ge(rot_ready, n)

            def newton(v, sd, r, t):
                link(dve.reciprocal(r, sd))
                link(dve.tensor_tensor(t, r, r, ALU.mult))
                link(dve.scalar_tensor_tensor(out=t, in0=t, scalar=-0.5, in1=v, op0=ALU.mult, op1=ALU.mult))
                return dve.scalar_tensor_tensor(out=r, in0=t, scalar=1.5, in1=r, op0=ALU.add, op1=ALU.mult)

            def row_rms(n, n_sq, r, pieces, meanwhile=None):
                dve.wait_ge(sq_ready, n_sq)
                link(dve.tensor_reduce(nt, ssq[:, :, 0:pieces], AXX, ALU.add))
                dve.tensor_scalar(var, nt, 1.0 / D, RMS_EPS, ALU.mult, ALU.add).then_inc(var_ready, 1)
                if meanwhile:
                    meanwhile()
                dve.wait_ge(std_ready, n)
                return newton(var, std, r, nt)

            def max_of_scores(l, kind, h):
                j = job_no(l, kind, h)
                r = 2 * (j % 4)
                if kind == "fox":
                    t = t_wait(dve, ("N", l, h))
                    step(dve.scalar_tensor_tensor(out=nfox[:, 0:P], in0=t[:, 0:P], scalar=cum[:, 0, h:h + 1],
                                                  in1=mask[:, 0:P], op0=ALU.subtract, op1=ALU.add))
                    dve.scalar_tensor_tensor(out=nfox[:, P:3 * P], in0=t[:, 0:S], scalar=cum[:, 1, h:h + 1],
                                             in1=mask[:, P:3 * P], op0=ALU.subtract,
                                             op1=ALU.add).then_inc(decay_ready, 1)
                    dve.wait_ge(decay_ready, HF * l + h + 1)
                if kind == "ali":
                    link(dve.tensor_scalar(nfox, dist, 2.0 ** (-8.0 * (h + 1) / H2), None, ALU.mult))
                dve.wait_ge(s_full, s_no[("job", j)] + 1)
                if kind == "mem":
                    link(dve.tensor_reduce(mx[:, r:r + 2], sbank[:, :].rearrange("p (s k) -> p s k", s=ST),
                                           AXX, ALU.max))
                else:
                    if j >= 2:
                        t_wait(dve, ("P", j - 2))
                    n0, n1 = (ndsa[:, 0:P], ndsa[:, S:2 * S]) if kind == "dsa" else (nfox[:, 0:P], nfox[:, P:3 * P])
                    scale = SCALE if kind == "dsa" else 1.0
                    step(dve.tensor_tensor_reduce(sc[:, j % 2, 0, 0:P], sbank[:, 0:P], n0, scale, -3e38,
                                                  ALU.subtract, ALU.max, mx[:, r:r + 1]))
                    link(dve.tensor_tensor_reduce(sc[:, j % 2, 1, :], sbank[:, S:2 * S], n1, scale, -3e38,
                                                  ALU.subtract, ALU.max, mx[:, r + 1:r + 2]))
                dve.tensor_scalar(nmx[:, r:r + 2], mx[:, r:r + 2], -1.0, None, ALU.mult).then_inc(m_ready, 1)

            def row_sums(l, kind, h):
                j = job_no(l, kind, h)
                r = 2 * (j % 4)
                dve.wait_ge(e_ready, j + 1)
                dve.reciprocal(rinv[:, r:r + 2], rs[:, r:r + 2]).then_inc(r_ready, 1)

            def gate(l, kind, h):
                if kind == "ali":
                    return
                j = job_no(l, kind, h)
                dve.wait_ge(o_full, o_no[("job", j)] + 1)
                dve.wait_ge(g_ready, gates_out(l, kind, h // 2))
                if j >= 2:
                    dve.wait_ge(yt_ready, j - 1)
                g = gmT if kind == "mem" else gT
                dve.tensor_tensor(y[:, j % 2, :], obank[:, 0:S], g[:, h, :], ALU.mult).then_inc(y_ready, 1)

            def y_low(l, kind, h):
                j, n = job_no(l, kind, h), tile_of(kind, h)
                dve.wait_ge(yhi_ready, j + 1)
                src = obank[:, 0:S] if kind == "ali" else y[:, j % 2, :]
                dve.tensor_tensor(yl[:, n, :], src, yh[:, n, :].bitcast(F32), ALU.subtract).then_inc(yt_ready, 1)

            def attention(l, b, table):
                if b - 1 in table:
                    row_sums(l, *table[b - 1])
                at = b - (4 if table is SCORES2 else 5)
                if at in table:
                    y_low(l, *table[at])
                if b - 3 in table:
                    gate(l, *table[b - 3])
                if b in table:
                    max_of_scores(l, *table[b])

            for u in range(8):
                unit_low(("memT", u), yh[:, 2 * u:2 * u + 2, :], yl[:, 2 * u:2 * u + 2, :], u + 1)
                if u % 2:
                    low_block(u // 2)

            def mem_side(b):
                if 8 <= b < 24 and b % 2 == 1:
                    u = (b - 8) // 2
                    unit_low(("xT", u), xh[:, 2 * u:2 * u + 2, :], xl[:, 2 * u:2 * u + 2, :], 8 + u + 1)

            slots(low_block, mem_side, 0, LAYER0, 4)
            last_sides(low_block, mem_side, 0, LAYER0)

            dve.wait_ge(tables_landed, 32)
            g1, b1 = (params[:, PARAM[k][0] + KT:PARAM[k][0] + 2 * KT] for k in ("gain", "bias"))
            gp = params[:, PARAM["gpre"][0]:PARAM["gpre"][1]]
            step(dve.tensor_tensor(gb, g1, gp, ALU.mult))
            link(dve.tensor_tensor(bb, b1, gp, ALU.mult))

            def residual(l, c):
                at = x[:, :, CW * c:CW * c + CW]
                if c == 0:
                    dve.wait_ge(rows_landed, 32 * (l + 1))
                row = [q[:, CW * c:CW * c + CW].unsqueeze(1).broadcast_to([P, ST, CW]) for q in (row_g, row_b)]
                t_wait(dve, ("nT", l, 2 * c + 1))
                link(dve.tensor_tensor(at, at, row[0], ALU.mult))
                dve.tensor_tensor(at, at, row[1], ALU.add).then_inc(xres_ready, 1)
                dve.wait_ge(xres_ready, 4 * l + c + 1)

            for l in range(DEPTH):
                g0 = LAYER0 + LAYER_SLOTS * l
                last = [0]

                def add_residual(n, l=l):
                    c = by[("o", l, n)]
                    col, width = COLS[n]
                    at = x[:, :, col:col + width]
                    acc_done(c)
                    dve.scalar_tensor_tensor(out=at, in0=at, scalar=ALPHA, in1=accs(c), op0=ALU.mult,
                                             op1=ALU.add).then_inc(sum_ready, 1)
                    dve.wait_ge(sum_ready, sums("o", l, n))
                    for c0 in range(0, width, 256):
                        for s in range(ST):
                            last[0] = step(dve.bn_stats(stats[:, s, (col + c0) // 256, :], at[:, s, c0:c0 + 256]))

                def layer_side(b, l=l, g0=g0):
                    name = ends(g0 + b, "iq", "dq", "dk", "o")
                    if l >= 1 and b in (18, 22, 26, 30):
                        residual(l - 1, (b - 18) // 4)
                    if b == 10:
                        dve.wait_ge(nar_ready, l + 1)
                        half = IDIM // 2
                        ra, rb = rot_a[0:IDIM, 0, :], rot_b[0:IDIM, 0, :]
                        step(dve.tensor_tensor(ra, y[0:IDIM, 1, :], tcos[0:IDIM], ALU.mult))
                        step(dve.tensor_tensor(rb[0:half], y[half:IDIM, 1, :], tsin[half:IDIM], ALU.mult))
                        link(dve.tensor_tensor(rb[half:IDIM], y[0:half, 1, :], tsin[0:half], ALU.mult))
                        dve.tensor_tensor(ikT[0:IDIM], ra, rb, ALU.add)
                        dve.tensor_tensor(ikT[IDIM:P], ra, rb, ALU.add).then_inc(ikt_ready, 1)
                        dve.wait_ge(ikt_ready, l + 1)
                    if b == 11:
                        t = t_wait(dve, ("nar", l))[:, 0:S].rearrange("p (s n) -> p s n", s=ST)
                        bf = params[:, PARAM["bf"][0] + HF * l:PARAM["bf"][0] + HF * l + HF]
                        link(dve.tensor_tensor(fz, t[:, :, IDIM + IH:NAR],
                                               bf.unsqueeze(1).broadcast_to([P, ST, HF]), ALU.add))
                        dve.scalar_tensor_tensor(out=fe, in0=fz, scalar=-1.0, in1=fz, op0=ALU.mult,
                                                 op1=ALU.min).then_inc(flog_in, 1)
                        dve.tensor_scalar(wi, t[:, :, IDIM:IDIM + IH], IH ** -0.5, None, ALU.mult).then_inc(wi_ready, 1)
                        dve.wait_ge(wi_ready, l + 1)
                    if b == 12:
                        dve.wait_ge(flog_ln, l + 1)
                        dve.scalar_tensor_tensor(out=logf, in0=fz, scalar=0.0, in1=fl, op0=ALU.min,
                                                 op1=ALU.subtract).then_inc(logf_ready, 1)
                    if b == 15:
                        t = t_wait(dve, ("cum", l))
                        dve.tensor_copy(flat(cum), t[:, 0:2 * HF]).then_inc(cum_ready, 1)
                        dve.wait_ge(cum_ready, l + 1)
                    if name and name[0] in ("iq", "dq", "dk"):
                        rope(name)
                    if IDX_AT <= b < IDX_AT + 6:
                        index_sum(l, b - IDX_AT)
                    if TOPK_AT <= b < TOPK_AT + TOPK // 8:
                        select_round(b - TOPK_AT)
                    if b == TOPK_AT + TOPK // 8 + 1:
                        for s, n in ((0, P), (1, S)):
                            link(dve.tensor_scalar(ndsa[:, s * S:s * S + n], itaken[:, s, 0:n], TAKEN / 1.5, BIG,
                                                   ALU.is_ge, ALU.mult))
                            link(dve.tensor_tensor(ndsa[:, s * S:s * S + n], ndsa[:, s * S:s * S + n],
                                                   mask[:, P * s:P * s + n], ALU.add))
                    attention(l, b, SCORES)
                    if name and name[0] == "o" and name[1] == l:
                        add_residual(name[2])

                def index_sum(l, f):
                    s, n, heads = index_shape(f)
                    if f:
                        dve.wait_ge(rel_used, 6 * l + f)
                    dve.wait_ge(rel_ready, 2 * (6 * l + f) + 2)
                    done = []
                    for c in range(len(heads) // 2):
                        for e, dst in ((0, iscore), (1, itaken)):
                            h = heads[2 * c + e]
                            src, w = rel[f % 2][e][:, c * n:c * n + n], wi[:, s, h:h + 1]
                            if len(done) >= 2:
                                dve.wait_ge(dve_done, done[-2])
                            if h < 2:
                                ins = dve.tensor_scalar(dst[:, s, 0:n], src, w, None, ALU.mult)
                            else:
                                ins = dve.scalar_tensor_tensor(out=dst[:, s, 0:n], in0=src, scalar=w,
                                                               in1=dst[:, s, 0:n], op0=ALU.mult, op1=ALU.add)
                            if c == len(heads) // 2 - 1 and e == 1:
                                ins.then_inc(rel_used, 1)
                            else:
                                done.append(step(ins))
                    dve.wait_ge(dve_done, done[-1])

                def select_round(r, l=l):
                    both = ((0, P), (1, S))
                    if r == 0:
                        dve.wait_ge(rel_used, 6 * l + 6)
                        for s, n in both:
                            step(dve.tensor_tensor(iscore[:, s, 0:n], iscore[:, s, 0:n], itaken[:, s, 0:n], ALU.add))
                        dve.wait_ge(dve_done, n_done[0])
                        for s, n in both:
                            step(dve.tensor_tensor(iscore[:, s, 0:n], iscore[:, s, 0:n], mask[:, P * s:P * s + n],
                                                   ALU.subtract))
                        dve.wait_ge(dve_done, n_done[0])
                    src = iscore if r == 0 else itaken
                    for s, n in both:
                        step(dve.max(top8[:, s, :], src[:, s, 0:n]))
                    dve.wait_ge(dve_done, n_done[0])
                    for s, n in both:
                        step(dve.match_replace(itaken[:, s, 0:n], top8[:, s, :], src[:, s, 0:n], TAKEN))
                    dve.wait_ge(dve_done, n_done[0])

                slots(low_block, layer_side, g0, LAYER_SLOTS, TURN if l else LEAD)
                last_sides(low_block, layer_side, g0, LAYER_SLOTS, LEAD - 1)
                nxt = g0 + LAYER_SLOTS
                add_residual(NC - 1)
                dve.wait_ge(dve_done, last[0])
                for s in range(ST):
                    step(dve.bn_aggr(mv[:, s, :], stats[:, s, :, :].rearrange("p c k -> p (c k)")))
                dve.wait_ge(dve_done, n_done[0])
                dve.tensor_scalar(var, mv[:, :, 1], LN_EPS, None, ALU.add).then_inc(var_ready, 1)
                dve.wait_ge(std_ready, l + 1)
                link(newton(var, std, rstd, nt))
                dve.scalar_tensor_tensor(out=nmr, in0=mv[:, :, 0], scalar=-1.0, in1=rstd, op0=ALU.mult,
                                         op1=ALU.mult).then_inc(nmr_ready, 1)

                def affine(n):
                    st, u = divmod(n, 8)
                    t = t_wait(dve, ("nT", st, u))
                    g, b_ = (gb, bb) if st else (param("gain", 0, KT), param("bias", 0, KT))
                    if u >= 4:
                        dve.wait_ge(xt_ready, 16 + n - 3)
                    for dt in range(2):
                        kt = 2 * u + dt
                        ins = dve.tensor_scalar(cb[:, u % 4, dt * S:dt * S + S], t[:, dt * S:dt * S + S],
                                                g[:, kt:kt + 1], b_[:, kt:kt + 1], ALU.mult, ALU.add)
                    ins.then_inc(aff_ready, 1)

                affine(8 * l)
                for u in range(8):
                    if u < 7:
                        affine(8 * l + u + 1)
                    dve.wait_ge(hi_ready, 16 + 8 * l + u + 1)
                    dve.tensor_tensor(flat(xl[:, 2 * u:2 * u + 2, :]), cb[:, u % 4, :],
                                      flat(xh[:, 2 * u:2 * u + 2, :]).bitcast(F32), ALU.subtract).then_inc(xt_ready, 1)
                    low_block(nxt + 2 + u)

            def ff_sum(name, turn):
                n, c = name[2], by[name]
                acc_done(c, turn)
                for s in range(ST):
                    rows = mixed_cols(n)[:, s, :]
                    ins = dve.scalar_tensor_tensor(out=rows, in0=accs(c)[:, s, :], scalar=sq3[:, s:s + 1], in1=rows,
                                                   op0=ALU.mult, op1=ALU.add)
                ins.then_inc(sum_ready, 1)
                dve.wait_ge(sum_ready, NC * turn + sums(*name))

            def mix_sum(name):
                c = by[name]
                acc_done(c)
                if name[0] == "oa":
                    ins = dve.tensor_copy(mixed[name[1]], accs(c))
                else:
                    rows = mixed_cols(name[1])
                    ins = dve.tensor_tensor(rows, rows, accs(c), ALU.add)
                ins.then_inc(sum_ready, 1)
                dve.wait_ge(sum_ready, sums(*name))

            def gain_rows(n, row, n_sq):
                dve.wait_ge(sq_ready, n_sq)
                col, width = COLS[n]
                g = row[:, col:col + width].unsqueeze(1).broadcast_to([P, ST, width])
                link(dve.tensor_tensor(mixed_cols(n), mixed_cols(n), g, ALU.mult))

            def add_rows(u, n, r, ready):
                for s in range(ST):
                    at = x[:, s, 256 * u:256 * (u + n)]
                    rows = mixed[u // 2][:, s, 256 * (u % 2):256 * (u % 2 + n)]
                    ins = dve.scalar_tensor_tensor(out=at, in0=rows, scalar=r[:, s:s + 1], in1=at,
                                                   op0=ALU.mult, op1=ALU.add)
                ins.then_inc(ready, 1)

            def conv_op(k):
                m, k2 = divmod(k, 2 * TAPS)
                tap, ct = k2 // 2, 2 * m + k2 % 2
                src, w = hT[:, ct, tap:tap + S], param("wdw", TAPS * ct + tap)
                if tap == 0:
                    if k2 == 0:
                        dve.wait_ge(hT_ready, m + 1)
                    ins = dve.tensor_scalar(cv[:, ct, :], src, w, param("bdw", ct), ALU.mult, ALU.add)
                else:
                    dve.wait_ge(conv_step, k - 1)
                    ins = dve.scalar_tensor_tensor(out=cv[:, ct, :], in0=src, scalar=w, in1=cv[:, ct, :],
                                                   op0=ALU.mult, op1=ALU.add)
                ins.then_inc(conv_step, 1)

            def block2_side(b):
                name = ends(BLOCK2 + b, "val", "gt", "q2", "k2")
                if b == 0:
                    link(dve.memset(hT[:, :, 0:PAD], 0.0))
                if b in (7, 9, 11, 13):
                    residual(1, (b - 7) // 2)
                if b == 16:
                    row_rms(3, 8, rstd2, 4).then_inc(rs_ready, 1)
                if b == 18:
                    t = t_wait(dve, ("rT",))
                    step(dve.tensor_copy(rT, t[:, 0:S]))
                    dve.tensor_scalar(rqT, t[:, 0:S], SCALE, None, ALU.mult).then_inc(rt_ready, 1)
                    dve.wait_ge(rt_ready, 1)
                if name:
                    k, m = name
                    c = by[name]
                    if k == "gt" and m >= 2:
                        dve.wait_ge(hT_ready, m - 1)
                    acc_done(c)
                    pair = slice(2 * m, 2 * m + 2)
                    dst = {"val": hT[:, pair, PAD:PAD + S], "gt": gt_b[m % 2], "q2": q2T[:, pair, :],
                           "k2": k2T[:, pair, :]}[k]
                    r = (rqT if k == "q2" else rT).unsqueeze(1).broadcast_to([P, 2, S])
                    dve.tensor_tensor(dst, accs(c), r, ALU.mult).then_inc(vg2_ready if k in ("val", "gt") else qk2_ready, 1)
                if b in (25, 33, 41, 49):
                    m = (b - 25) // 8
                    dve.wait_ge(sig_ready, m + 1)
                    for i in range(2):
                        ct = 2 * m + i
                        at = hT[:, ct, PAD:PAD + S]
                        ins = dve.scalar_tensor_tensor(out=at, in0=at, scalar=param("bglu", ct), in1=gt_b[m % 2][:, i, :],
                                                       op0=ALU.add, op1=ALU.mult)
                    ins.then_inc(hT_ready, 1)
                attention(0, b, SCORES2)
                at = [max(0, n * CONV_PER_2_SLOTS // 2) for n in (b - CONV_AT, b - CONV_AT + 1)]
                for k in range(at[0], min(at[1], CONV_OPS)):
                    conv_op(k)
                if b in (84, 87, 90, 93):
                    n = (b - 84) // 3
                    mix_sum(("oa", n))
                if b == MEAN_AT:
                    dve.wait_ge(s_full, s_no[("cmean",)] + 1)
                    dve.scalar_tensor_tensor(out=cv, in0=sbank[:, 0:S].unsqueeze(1).broadcast_to([P, 8, S]),
                                             scalar=-1.0 / CONV, in1=cv, op0=ALU.mult, op1=ALU.add).then_inc(yc_ready, 1)
                if b == VAR_AT:
                    dve.wait_ge(s_full, s_no[("cvar",)] + 1)
                    dve.tensor_scalar(cvar_b, sbank[:, 0:S], 1.0 / CONV, LN_EPS, ALU.mult, ALU.add).then_inc(var_ready, 1)
                if b == VAR_AT + 1:
                    dve.wait_ge(std_ready, 4)
                    link(newton(cvar_b, cstd_b, crs_b, cnt_b))
                if SILU_AT - 1 <= b < SILU_AT + 3:
                    u = b - SILU_AT + 1
                    at = cv[:, 2 * u:2 * u + 2, :]
                    dve.tensor_tensor(at, at, crs_b.unsqueeze(1).broadcast_to([P, 2, S]), ALU.mult).then_inc(cn_ready, 1)
                if SILU_AT + 1 <= b < SILU_AT + 5:
                    u = b - SILU_AT - 1
                    at = slice(8 + 2 * u, 8 + 2 * u + 2)
                    dve.wait_ge(ch_ready, u + 1)
                    dve.tensor_tensor(yl[:, at, :], cv[:, 2 * u:2 * u + 2, :], yh[:, at, :].bitcast(F32),
                                      ALU.subtract).then_inc(ct_ready, 1)
                if b in (97, 102, 107, 112, 117):
                    mix_sum(("ob", (b - 97) // 5))
                if b in (99, 104, 109, 114, 119):
                    n = (b - 99) // 5
                    if n == 0:
                        dve.wait_ge(rowp_landed, 16)
                    gain_rows(n, rowp, 8 + 2 * (n + 1))

            slots(low_block, block2_side, BLOCK2, BLOCK2_SLOTS, TURN)
            last_sides(low_block, block2_side, BLOCK2, BLOCK2_SLOTS, LEAD - 1)
            mix_sum(("ob", NC - 1))
            low_block(FF0 + 2)
            n_sq = 8 + 2 * NC
            link(row_rms(5, n_sq, rstdm, NC, lambda: gain_rows(NC - 1, rowp, n_sq)))
            add_rows(0, 1, rstdm, norm_ready)
            add_rows(1, 1, rstdm, norm_ready)
            for u in range(8):
                t = t_wait(dve, ("h2T", u))
                dve.wait_ge(hi_ready, 32 + u + 1)
                for dt in range(2):
                    kt = 2 * u + dt
                    ins = dve.scalar_tensor_tensor(out=xl[:, kt, :], in0=t[:, dt * S:dt * S + S],
                                                   scalar=param("gffn", kt), in1=xh[:, kt, :].bitcast(F32),
                                                   op0=ALU.mult, op1=ALU.subtract)
                ins.then_inc(xt_ready, 1)
                if u in (1, 2, 4):
                    add_rows({1: 2, 2: 4, 4: 6}[u], 2, rstdm, norm_ready)
                if u >= 1:
                    low_block(FF0 + 2 + u)

            def ff_side(b, q, turn=0):
                name = ends(FF0 + FF_SLOTS * q + b, "f1", "f2")
                if q == 0 and b == 18:
                    link(row_rms(6, 16 + 2 * NC, rstd3, 4))
                    link(dve.tensor_tensor(sq3, rstd3, rstd3, ALU.mult))
                if q == 0 and b in (20, 24, 28, 32):
                    link(dve.memset(mixed[(b - 20) // 4], 0.0))
                if name and name[0] == "f1":
                    n, j = 8 * name[1] + name[2], name[2]
                    dve.wait_ge(yhi_ready, 8 * turn + 40 + n + 1)
                    dve.tensor_tensor(flat(yl[:, 2 * j:2 * j + 2, :]), cb[:, j % 4, :],
                                      flat(yh[:, 2 * j:2 * j + 2, :]).bitcast(F32), ALU.subtract).then_inc(yt_ready, 1)
                if name and name[0] == "f2":
                    ff_sum(name, turn)

            slots(low_block, lambda b: ff_side(b, 0), FF0, FF_SLOTS, TURN)
            with dve.Fori(0, NQ - 1) as turn:
                slots(lambda g: low_block(g, turn), lambda b: ff_side(b, 1, turn), FF0 + FF_SLOTS, FF_SLOTS, 0)
            dve.wait_ge(rowf_landed, 16)
            n_sq = 16 + 2 * NC
            for n in range(NC - 1):
                gain_rows(n, rowf, n_sq + 2 * (n + 1))
            ff_sum(("f2", NQ - 1, NC - 1), 0)
            n_sq += 2 * NC
            link(row_rms(7, n_sq, rstd4, NC, lambda: gain_rows(NC - 1, rowf, n_sq)))
            for c in range(4):
                add_rows(2 * c, 2, rstd4, fin_ready)

        @block.sync
        def _(sp):
            sp.dma_start(ident, a["consts"][:, 0:P]).then_inc(ident_landed, 16)
            mem_rows = a["mem"][0].rearrange("(s p) d -> p s d", p=P)
            def load(g, rows, col, turn=0):
                if g >= RING:
                    low_taken(sp, g - RING, turn)
                c = chunk_at[g][0]
                dst, landed_in = part(raw, g), raw_landed[g % RING]
                if c.name[0] == "nar":
                    sp.dma_start(dst[:, :, 0:IDIM + IH], rows[:, :, C_IK:C_IK + IDIM + IH]).then_inc(landed_in, 16)
                    sp.dma_start(dst[:, :, IDIM + IH:NAR], rows[:, :, C_FL:C_FL + HF]).then_inc(landed_in, 16)
                else:
                    sp.dma_start(dst, rows[:, :, bass.ds(col, c.width)]).then_inc(landed_in, 16)

            for g in range(FF0 + FF_SLOTS):
                if g < 4:
                    at = slice(CW * g, CW * g + CW)
                    sp.dma_start(x[:, :, at], mem_rows[:, :, at]).then_inc(mem_landed[g], 16)
                c, i = chunk_at[g]
                r0 = c.row0 + c.nk * P * i
                load(g, c.w[r0:r0 + c.nk * P, :].rearrange("(t p) n -> p t n", p=P), c.col)
            with sp.Fori(0, NQ - 1) as turn:
                for g in range(FF0 + FF_SLOTS, FF0 + 2 * FF_SLOTS):
                    c, i = chunk_at[g]
                    r0 = c.row0 + c.nk * P * i
                    if c.name[0] == "f1":
                        load(g, c.w[r0:r0 + c.nk * P, :].rearrange("(t p) n -> p t n", p=P), D * turn + c.col, turn)
                    else:
                        rows = c.w[bass.ds(D * turn + r0, c.nk * P), :]
                        load(g, rows.rearrange("(t p) n -> p t n", p=P), c.col, turn)
            rows_out = out[0].rearrange("(s p) d -> p s d", p=P)
            for c in range(4):
                sp.wait_ge(fin_ready, c + 1)
                at = slice(CW * c, CW * c + CW)
                sp.dma_start(rows_out[:, :, at], x[:, :, at]).then_inc(out_done, 16)
            sp.wait_ge(out_done, 64)

        @block.gpsimd
        def _(pool):
            t_wait(pool, ("memT", 6))
            t_wait(pool, ("memT", 7))
            x_rows = a["x"][0].rearrange("(s p) d -> p s d", p=P)
            for c in range(4):
                pool.wait_ge(block_used, 2 * c + 2)
                at = slice(CW * c, CW * c + CW)
                pool.dma_start(x[:, :, at], x_rows[:, :, at]).then_inc(x_landed[c], 16)
            pool.wait_ge(block_used, 12)
            pool.dma_start(params[:, :], a["params"]).then_inc(tables_landed, 16)
            pool.dma_start(consts[:, P:N_CONST], a["consts"][:, P:N_CONST]).then_inc(tables_landed, 16)
            for l in range(DEPTH):
                for g in pool_blocks[l]:
                    low_part(pool, g, low_pool)
                pool.wait_ge(block_used, by[("o", l, NC - 1)].blocks[-1] + 1)
                pool.dma_start(row_g, a["ln_gain"][l].partition_broadcast(P)).then_inc(rows_landed, 16)
                pool.dma_start(row_b, a["ln_bias"][l].partition_broadcast(P)).then_inc(rows_landed, 16)
            for g in pool_blocks[DEPTH]:
                low_part(pool, g, low_pool)
            pool.wait_ge(o_full, o_no[("job", job_no(0, "ali", H2 - 1))] + 1)
            pool.dma_start(rowp, a["g_mix_post_2"][0].partition_broadcast(P)).then_inc(rowp_landed, 16)
            pool.wait_ge(ct_ready, 4)
            pool.dma_start(rowf, a["g_ffn_post_2"][0].partition_broadcast(P)).then_inc(rowf_landed, 16)


_WHOLE = ["x", "mem", "w_in", "w_mem_kv", "w_out", "ln_gain", "ln_bias", "w_in_2", "w_out_2", "g_mix_post_2",
          "w_ff1_2", "w_ff2_2", "g_ffn_post_2"]


def tables():
    f = np.float32
    i, j = np.arange(P)[:, None], np.arange(P)[None, :]
    after = (j > i).astype(f)
    out = {"ident": np.eye(P, dtype=f)}
    out["mask"] = np.concatenate([after, np.zeros((P, P), f), after], 1) * f(BIG)
    out["upto"] = np.concatenate([(i <= j).astype(f), np.ones((P, P), f)], 1)
    for d in (HD, IDIM):
        half = d // 2
        freq = f(10000.0) ** (-np.arange(half, dtype=f) / f(half))
        ang = np.arange(S).astype(f)[:, None] * freq[None, :]
        cos, sin = np.cos(ang), np.sin(ang)
        turned = [np.tile(np.concatenate(p, 1).T, (P // d, 1)) for p in ((cos, cos), (sin, -sin))]
        if d == HD:
            out["cos"], out["sin"] = turned
        else:
            out["tcos"], out["tsin"] = turned
    far = after * f(1e33)
    out["dist"] = np.concatenate([np.abs(i - j) + far, P + i - j, np.abs(i - j) + far], 1)
    return np.ascontiguousarray(np.concatenate([out[k] for k in CONST], 1), dtype=f)


def kernel(**inputs):
    import concourse.bacc as bacc
    from concourse.bass_utils import run_bass_kernel_spmd

    v = {k: np.asarray(a) for k, a in inputs.items()}

    def cols(a):
        return a.reshape(-1, P).T

    parts = {
        "gain": cols(v["ln_gain"]), "bias": cols(v["ln_bias"]), "gpre": cols(v["g_mix_pre_2"]),
        "gffn": cols(v["g_ffn_pre_2"]), "bf": np.broadcast_to(v["b_forget"].reshape(1, -1), (P, DEPTH * HF)),
        "bglu": cols(v["b_glu_2"]), "bdw": cols(v["b_dw_2"]), "cg": cols(v["ln_conv_g_2"]), "cb": cols(v["ln_conv_b_2"]),
        "wdw": v["w_dw_2"][0].reshape(TAPS, 8, P).transpose(2, 1, 0).reshape(P, 8 * TAPS),
    }
    arrays = {k: np.ascontiguousarray(v[k]) for k in _WHOLE}
    arrays["params"] = np.ascontiguousarray(np.concatenate([parts[k] for k in PARAM], 1))
    arrays["consts"] = tables()

    nc = bacc.Bacc("TRN2", target_bir_lowering=False, num_devices=1)
    aps = {k: nc.dram_tensor(f"in_{k}", a.shape, F32, kind="ExternalInput").ap() for k, a in arrays.items()}
    out = nc.dram_tensor("out", v["x"].shape, F32, kind="ExternalOutput").ap()
    build(nc, aps, out)
    r = run_bass_kernel_spmd(nc, [{f"in_{k}": a for k, a in arrays.items()}], core_ids=[0])
    return r.results[0]["out"]
```
